# Optimizing a Trainium2 kernel written in Bass

```python
import math
import jax, jax.numpy as jnp
from jax import lax
import numpy as np

D_MODEL = 1024
BATCH = 1
SEQ = 1024
DEPTH = 1
DEC_BATCH = 8
DEC_SEQ = 8
PAST_LEN = 1024
PAGE_SIZE = 128

HEAD_DIM = 64
NSA_HEADS = 8
NSA_KV_HEADS = 2
NSA_GROUP = NSA_HEADS // NSA_KV_HEADS
CMP_BLOCK = 32
CMP_STRIDE = 16
CMP_HIDDEN = 2 * HEAD_DIM
SEL_BLOCK = 64
N_SELECT = 16
WINDOW = 512
FOX_HEADS = 8
N_BUCKETS = 32
MAX_DISTANCE = 128
D_FF = 2816
CONV_W = 3
PLE_DIM = 256
Q_BLOCK = 128
ALPHA = (2.0 * DEPTH) ** 0.25
BETA = (8.0 * DEPTH) ** -0.25
LN_EPS = 1e-5
NSA_Q_W = NSA_HEADS * HEAD_DIM
NSA_KV_W = NSA_KV_HEADS * HEAD_DIM
NSA_GATE_W = NSA_HEADS * 3
FOX_W = FOX_HEADS * HEAD_DIM
IN_SPLITS = (NSA_Q_W, 6 * NSA_KV_W, NSA_GATE_W, FOX_W, FOX_W, FOX_W, FOX_HEADS, D_MODEL, D_MODEL)
D_IN = sum(IN_SPLITS)

kernel_name = "hybrid_nsa_fox_decoder_step"

def layer_norm(x, g, b):
    xf = x.astype(jnp.float32)
    mu = jnp.mean(xf, axis=-1, keepdims=True)
    var = jnp.mean(jnp.square(xf - mu), axis=-1, keepdims=True)
    y = (xf - mu) * lax.rsqrt(var + LN_EPS) * g.astype(jnp.float32) + b.astype(jnp.float32)
    return y.astype(x.dtype)

def masked_softmax(logits, mask):
    l = jnp.where(mask, logits.astype(jnp.float32), -jnp.inf)
    m = jnp.max(l, axis=-1, keepdims=True)
    m = jnp.where(jnp.isfinite(m), m, 0.0)
    e = jnp.where(mask, jnp.exp(l - m), 0.0)
    return e / jnp.maximum(jnp.sum(e, axis=-1, keepdims=True), 1e-30)

def t5_bucket(dist):
    n = jnp.maximum(dist, 0)
    max_exact = N_BUCKETS // 2
    nf = jnp.maximum(n, 1).astype(jnp.float32)
    large = max_exact + (jnp.log(nf / max_exact) / math.log(MAX_DISTANCE / max_exact)
                         * (N_BUCKETS - max_exact)).astype(jnp.int32)
    large = jnp.minimum(large, N_BUCKETS - 1)
    return jnp.where(n < max_exact, n, large)

def to_blocks(a):
    B, T = a.shape[:2]
    return jnp.swapaxes(a.reshape((B, T // Q_BLOCK, Q_BLOCK) + a.shape[2:]), 0, 1)

def from_blocks(a):
    a = jnp.swapaxes(a, 0, 1)
    return a.reshape((a.shape[0], a.shape[1] * a.shape[2]) + a.shape[3:])

def gather_pages(cache, page_table):
    g = cache[page_table]
    return g.reshape((g.shape[0], g.shape[1] * g.shape[2]) + g.shape[3:])

def project(h, w_in, b_forget):
    B, T, _ = h.shape
    z = h @ w_in
    idx = np.cumsum(IN_SPLITS)[:-1].tolist()
    nq, nkv, ng, fq, fk, fv, ff, ga, gb = jnp.split(z, idx, axis=-1)
    nq = nq.reshape(B, T, NSA_KV_HEADS, NSA_GROUP, HEAD_DIM)
    nkv = nkv.reshape(B, T, 6, NSA_KV_HEADS, HEAD_DIM)
    ng = jax.nn.sigmoid(ng.reshape(B, T, NSA_KV_HEADS, NSA_GROUP, 3))
    fq = fq.reshape(B, T, FOX_HEADS, HEAD_DIM)
    fk = fk.reshape(B, T, FOX_HEADS, HEAD_DIM)
    fv = fv.reshape(B, T, FOX_HEADS, HEAD_DIM)
    logf = jax.nn.log_sigmoid((ff + b_forget).astype(jnp.float32))
    return nq, nkv, ng, fq, fk, fv, logf, ga, gb

def compress(raw, pe, w1, w2):
    T = raw.shape[1]
    n_c = (T - CMP_BLOCK) // CMP_STRIDE + 1
    idx = np.arange(n_c)[:, None] * CMP_STRIDE + np.arange(CMP_BLOCK)[None, :]
    blocks = raw[:, idx] + pe[None, None, :, None, :]
    hid = jax.nn.gelu(jnp.einsum('bnlhd,ldk->bnhk', blocks, w1))
    return jnp.einsum('bnhk,kd->bnhd', hid, w2), jnp.asarray(idx[:, -1], dtype=jnp.int32)

def sel_blocks(raw):
    B, T = raw.shape[:2]
    n_sel = -(-T // SEL_BLOCK)
    raw = jnp.pad(raw, ((0, 0), (0, n_sel * SEL_BLOCK - T), (0, 0), (0, 0)))
    return raw.reshape(B, n_sel, SEL_BLOCK, NSA_KV_HEADS, HEAD_DIM)

def nsa_prepare(rows, W):
    kc, cpos = compress(rows[:, :, 0], W['nsa_cmp_pe'][0], W['nsa_cmp_w1'][0], W['nsa_cmp_w2'][0])
    vc, _ = compress(rows[:, :, 1], W['nsa_cmp_pe'][1], W['nsa_cmp_w1'][1], W['nsa_cmp_w2'][1])
    ks = sel_blocks(rows[:, :, 2])
    vs = sel_blocks(rows[:, :, 3])
    n_c, n_sel = kc.shape[1], ks.shape[1]
    start = np.arange(n_c)[:, None] * CMP_STRIDE
    j = np.arange(n_sel)[None, :]
    ov = jnp.asarray((start < (j + 1) * SEL_BLOCK) & (start + CMP_BLOCK > j * SEL_BLOCK), dtype=jnp.float32)
    return kc, vc, cpos, ks, vs, ov

def nsa_block(q, qpos, g, kc, vc, cpos, ks, vs, ov, kw, vw, wpos, tb):
    B, Tq = q.shape[:2]
    scale = HEAD_DIM ** -0.5
    dc = qpos[:, None] - cpos[None, :]
    lc = jnp.einsum('bthgd,bnhd->bhgtn', q, kc).astype(jnp.float32) * scale
    lc = lc + jnp.transpose(tb[t5_bucket(dc)], (2, 3, 0, 1))
    pc = masked_softmax(lc, dc >= 0)
    oc = jnp.einsum('bhgtn,bnhd->bthgd', pc.astype(vc.dtype), vc)
    n_sel = ks.shape[1]
    imp = jnp.einsum('bhgtn,nj->bhtj', pc, ov)
    blk = jnp.arange(n_sel, dtype=jnp.int32)[None, :]
    qblk = (qpos // SEL_BLOCK)[:, None]
    forced = (blk == 0) | (blk == qblk) | (blk == qblk - 1)
    imp = jnp.where(forced, jnp.inf, jnp.where(blk > qblk, -jnp.inf, imp))
    top_s, top_i = lax.top_k(imp, min(N_SELECT, n_sel))
    valid = top_s > -jnp.inf
    bi = jnp.arange(B)[:, None, None, None]
    hi = jnp.arange(NSA_KV_HEADS)[None, :, None, None]
    kg = jnp.transpose(ks, (0, 3, 1, 2, 4))[bi, hi, top_i]
    vg = jnp.transpose(vs, (0, 3, 1, 2, 4))[bi, hi, top_i]
    kpos = top_i[..., None] * SEL_BLOCK + jnp.arange(SEL_BLOCK, dtype=jnp.int32)
    ds = qpos[None, None, :, None, None] - kpos
    bias_s = jax.vmap(lambda tbh, bk: tbh[bk], in_axes=(1, 1), out_axes=1)(tb, t5_bucket(ds))
    ls = jnp.einsum('bthgd,bhtnsd->bhgtns', q, kg).astype(jnp.float32) * scale + jnp.moveaxis(bias_s, -1, 2)
    n_k = top_i.shape[-1] * SEL_BLOCK
    ms = (valid[..., None] & (ds >= 0)).reshape(B, NSA_KV_HEADS, 1, Tq, n_k)
    ps = masked_softmax(ls.reshape(B, NSA_KV_HEADS, NSA_GROUP, Tq, n_k), ms)
    osl = jnp.einsum('bhgtm,bhtmd->bthgd', ps.astype(vs.dtype), vg.reshape(B, NSA_KV_HEADS, Tq, n_k, HEAD_DIM))
    dw = qpos[:, None] - wpos[None, :]
    lw = jnp.einsum('bthgd,bshd->bhgts', q, kw).astype(jnp.float32) * scale
    lw = lw + jnp.transpose(tb[t5_bucket(dw)], (2, 3, 0, 1))
    pw = masked_softmax(lw, (dw >= 0) & (dw < WINDOW) & (wpos[None, :] >= 0))
    ow = jnp.einsum('bhgts,bshd->bthgd', pw.astype(vw.dtype), vw)
    return g[..., 0:1] * oc + g[..., 1:2] * osl + g[..., 2:3] * ow

def fox_block(q, qpos, cq, k, v, ck, kpos):
    scale = HEAD_DIM ** -0.5
    l = jnp.einsum('bthd,bshd->bhts', q, k).astype(jnp.float32) * scale
    l = l + jnp.transpose(cq, (0, 2, 1))[..., None] - jnp.transpose(ck, (0, 2, 1))[:, :, None, :]
    p = masked_softmax(l, kpos[None, :] <= qpos[:, None])
    return jnp.einsum('bhts,bshd->bthd', p.astype(v.dtype), v)

def merge(o_nsa, o_fox, ga, gb, W):
    B, T = o_nsa.shape[:2]
    a = o_nsa.reshape(B, T, NSA_Q_W) @ W['w_branch_a']
    b = o_fox.reshape(B, T, FOX_W) @ W['w_branch_b']
    return (jax.nn.sigmoid(ga) * a + jax.nn.sigmoid(gb) * b) @ W['w_out']

def finish_layer(x, mix, p_emb, conv_prev, W):
    x = layer_norm(ALPHA * x + mix, W['ln1_g'], W['ln1_b'])
    T = x.shape[1]
    u = x @ W['w_ffn_up']
    ext = jnp.concatenate([conv_prev.astype(u.dtype), u], axis=1)
    conv = W['ffn_conv_b'] + sum(W['ffn_conv_w'][k] * ext[:, k:k + T] for k in range(CONV_W))
    f = (jax.nn.gelu(conv) * (x @ W['w_ffn_gate'])) @ W['w_ffn_down']
    x = layer_norm(ALPHA * x + f, W['ln2_g'], W['ln2_b'])
    x = x + jax.nn.sigmoid(x @ W['w_ple_gate']) * (p_emb @ W['w_ple'])
    return x, ext[:, T:]

def prompt_layer(x, p_emb, W, tb):
    B, T = x.shape[:2]
    nq, nkv, ng, fq, fk, fv, logf, ga, gb = project(x, W['w_in'], W['b_forget'])
    kc, vc, cpos, ks, vs, ov = nsa_prepare(nkv[:, :, :4], W)
    kw_pad = jnp.pad(nkv[:, :, 4:], ((0, 0), (WINDOW, 0), (0, 0), (0, 0), (0, 0)))
    c = jnp.cumsum(logf, axis=1)
    kpos = jnp.arange(T, dtype=jnp.int32)

    def block(args):
        i, q_b, g_b, fq_b, c_b = args
        t0 = i * Q_BLOCK
        qpos = t0 + jnp.arange(Q_BLOCK, dtype=jnp.int32)
        kw_b = lax.dynamic_slice_in_dim(kw_pad, t0, WINDOW + Q_BLOCK, axis=1)
        wpos = t0 - WINDOW + jnp.arange(WINDOW + Q_BLOCK, dtype=jnp.int32)
        o_n = nsa_block(q_b, qpos, g_b, kc, vc, cpos, ks, vs, ov, kw_b[:, :, 0], kw_b[:, :, 1], wpos, tb)
        o_f = fox_block(fq_b, qpos, c_b, fk, fv, c, kpos)
        return o_n, o_f

    nb = T // Q_BLOCK
    o_n, o_f = lax.map(block, (jnp.arange(nb, dtype=jnp.int32), to_blocks(nq), to_blocks(ng),
                                to_blocks(fq), to_blocks(c)))
    mix = merge(from_blocks(o_n), from_blocks(o_f), ga, gb, W)
    y, conv_state = finish_layer(x, mix, p_emb, jnp.zeros((B, CONV_W - 1, D_FF), x.dtype), W)
    wb = min(WINDOW, T)
    return y, (jnp.stack([fk, fv], axis=2), logf, nkv[:, :, :4], nkv[:, T - wb:, 4:], conv_state)

def sample_layer(x, p_emb, c_fox_kv, c_fox_logf, c_nsa, win, conv_prev, page_table, W, tb):
    S = x.shape[1]
    nq, nkv, ng, fq, fk, fv, logf, ga, gb = project(x, W['w_in'], W['b_forget'])
    past_nsa = gather_pages(c_nsa, page_table)
    P = past_nsa.shape[1]
    qpos = P + jnp.arange(S, dtype=jnp.int32)
    kc, vc, cpos, ks, vs, ov = nsa_prepare(jnp.concatenate([past_nsa, nkv[:, :, :4]], axis=1), W)
    wb = win.shape[1]
    win_all = jnp.concatenate([win, nkv[:, :, 4:]], axis=1)
    wpos = P - wb + jnp.arange(wb + S, dtype=jnp.int32)
    o_n = nsa_block(nq, qpos, ng, kc, vc, cpos, ks, vs, ov, win_all[:, :, 0], win_all[:, :, 1], wpos, tb)
    past_fox = gather_pages(c_fox_kv, page_table)
    k_all = jnp.concatenate([past_fox[:, :, 0], fk], axis=1)
    v_all = jnp.concatenate([past_fox[:, :, 1], fv], axis=1)
    logf_all = jnp.concatenate([gather_pages(c_fox_logf, page_table).astype(jnp.float32), logf], axis=1)
    c = jnp.cumsum(logf_all, axis=1)
    o_f = fox_block(fq, qpos, c[:, P:], k_all, v_all, c, jnp.arange(P + S, dtype=jnp.int32))
    mix = merge(o_n, o_f, ga, gb, W)
    y, conv_state = finish_layer(x, mix, p_emb, conv_prev, W)
    return y, (jnp.stack([fk, fv], axis=2), logf, nkv[:, :, :4], win_all[:, S:], conv_state)

def setup_inputs(seed: int = 0) -> dict:
    key = jax.random.key(seed)
    ks = jax.random.split(key, 40)
    n_pages = PAST_LEN // PAGE_SIZE
    n_pool = (5 * DEC_BATCH * n_pages) // 4
    wb = min(WINDOW, PAST_LEN)

    def nrm(k, shape, s=1.0):
        return s * jax.random.normal(k, shape, jnp.float32)

    page_table = jax.random.permutation(ks[9], n_pool)[: DEC_BATCH * n_pages].reshape(DEC_BATCH, n_pages).astype(jnp.int32)
    return {
        "x_prompt": nrm(ks[0], (BATCH, SEQ, D_MODEL)),
        "x_sample": nrm(ks[1], (DEC_BATCH, DEC_SEQ, D_MODEL)),
        "p_prompt": nrm(ks[2], (DEPTH, BATCH, SEQ, PLE_DIM)),
        "p_sample": nrm(ks[3], (DEPTH, DEC_BATCH, DEC_SEQ, PLE_DIM)),
        "cache_fox_kv": nrm(ks[4], (DEPTH, n_pool, PAGE_SIZE, 2, FOX_HEADS, HEAD_DIM)),
        "cache_fox_logf": jax.nn.log_sigmoid(4.0 + nrm(ks[5], (DEPTH, n_pool, PAGE_SIZE, FOX_HEADS))),
        "cache_nsa_kv": nrm(ks[6], (DEPTH, n_pool, PAGE_SIZE, 4, NSA_KV_HEADS, HEAD_DIM)),
        "state_nsa_win": nrm(ks[7], (DEPTH, DEC_BATCH, wb, 2, NSA_KV_HEADS, HEAD_DIM)),
        "state_ffn_conv": nrm(ks[8], (DEPTH, DEC_BATCH, CONV_W - 1, D_FF)),
        "page_table": page_table,
        "w_in": nrm(ks[10], (DEPTH, D_MODEL, D_IN), D_MODEL ** -0.5),
        "b_forget": 4.0 + nrm(ks[11], (DEPTH, FOX_HEADS), 0.5),
        "nsa_cmp_pe": nrm(ks[12], (DEPTH, 2, CMP_BLOCK, HEAD_DIM), 0.1),
        "nsa_cmp_w1": nrm(ks[13], (DEPTH, 2, CMP_BLOCK, HEAD_DIM, CMP_HIDDEN), (CMP_BLOCK * HEAD_DIM) ** -0.5),
        "nsa_cmp_w2": nrm(ks[14], (DEPTH, 2, CMP_HIDDEN, HEAD_DIM), CMP_HIDDEN ** -0.5),
        "rel_bias": nrm(ks[15], (N_BUCKETS, NSA_HEADS), 0.5),
        "w_branch_a": nrm(ks[16], (DEPTH, NSA_Q_W, D_MODEL), NSA_Q_W ** -0.5),
        "w_branch_b": nrm(ks[17], (DEPTH, FOX_W, D_MODEL), FOX_W ** -0.5),
        "w_out": nrm(ks[18], (DEPTH, D_MODEL, D_MODEL), BETA * D_MODEL ** -0.5),
        "ln1_g": 1.0 + nrm(ks[19], (DEPTH, D_MODEL), 0.05),
        "ln1_b": nrm(ks[20], (DEPTH, D_MODEL), 0.02),
        "ln2_g": 1.0 + nrm(ks[21], (DEPTH, D_MODEL), 0.05),
        "ln2_b": nrm(ks[22], (DEPTH, D_MODEL), 0.02),
        "w_ffn_up": nrm(ks[23], (DEPTH, D_MODEL, D_FF), D_MODEL ** -0.5),
        "w_ffn_gate": nrm(ks[24], (DEPTH, D_MODEL, D_FF), D_MODEL ** -0.5),
        "ffn_conv_w": nrm(ks[25], (DEPTH, CONV_W, D_FF), CONV_W ** -0.5),
        "ffn_conv_b": nrm(ks[26], (DEPTH, D_FF), 0.02),
        "w_ffn_down": nrm(ks[27], (DEPTH, D_FF, D_MODEL), BETA * D_FF ** -0.5),
        "w_ple": nrm(ks[28], (DEPTH, PLE_DIM, D_MODEL), PLE_DIM ** -0.5),
        "w_ple_gate": nrm(ks[29], (DEPTH, D_MODEL, D_MODEL), D_MODEL ** -0.5),
    }

def reference(x_prompt, x_sample, p_prompt, p_sample, cache_fox_kv, cache_fox_logf, cache_nsa_kv,
              state_nsa_win, state_ffn_conv, page_table, w_in, b_forget, nsa_cmp_pe, nsa_cmp_w1,
              nsa_cmp_w2, rel_bias, w_branch_a, w_branch_b, w_out, ln1_g, ln1_b, ln2_g, ln2_b,
              w_ffn_up, w_ffn_gate, ffn_conv_w, ffn_conv_b, w_ffn_down, w_ple, w_ple_gate):
    tb = rel_bias.reshape(N_BUCKETS, NSA_KV_HEADS, NSA_GROUP)
    xp, xs = x_prompt, x_sample
    st_p, st_s = [], []
    for i in range(DEPTH):
        W = {
            'w_in': w_in[i], 'b_forget': b_forget[i], 'nsa_cmp_pe': nsa_cmp_pe[i],
            'nsa_cmp_w1': nsa_cmp_w1[i], 'nsa_cmp_w2': nsa_cmp_w2[i], 'w_branch_a': w_branch_a[i],
            'w_branch_b': w_branch_b[i], 'w_out': w_out[i], 'ln1_g': ln1_g[i], 'ln1_b': ln1_b[i],
            'ln2_g': ln2_g[i], 'ln2_b': ln2_b[i], 'w_ffn_up': w_ffn_up[i], 'w_ffn_gate': w_ffn_gate[i],
            'ffn_conv_w': ffn_conv_w[i], 'ffn_conv_b': ffn_conv_b[i], 'w_ffn_down': w_ffn_down[i],
            'w_ple': w_ple[i], 'w_ple_gate': w_ple_gate[i],
        }
        xp, sp = prompt_layer(xp, p_prompt[i], W, tb)
        xs, ss = sample_layer(xs, p_sample[i], cache_fox_kv[i], cache_fox_logf[i], cache_nsa_kv[i],
                              state_nsa_win[i], state_ffn_conv[i], page_table, W, tb)
        st_p.append(sp)
        st_s.append(ss)

    def stk(lst, j):
        return jnp.stack([s[j] for s in lst])

    return (xp, xs, stk(st_p, 0), stk(st_s, 0), stk(st_p, 1), stk(st_s, 1), stk(st_p, 2), stk(st_s, 2),
            stk(st_p, 3), stk(st_s, 3), stk(st_p, 4), stk(st_s, 4))


_drawn_inputs = setup_inputs


def setup_inputs(seed=0):
    import zlib

    import numpy as np

    out = dict(_drawn_inputs(seed))
    spreads = {}
    factors = {'cache_fox_logf': 8.0,
     'cache_nsa_kv': 3.882,
     'nsa_cmp_pe': 7.068,
     'rel_bias': 4.936,
     'ln1_b': 2.818,
     'ln2_b': 3.15,
     'ffn_conv_b': 8.0}
    for name, (base, spread) in spreads.items():
        noise = np.random.default_rng([zlib.crc32(name.encode()), seed]).standard_normal(out[name].shape)
        drawn = base * np.exp(spread * noise) if base else spread * noise
        out[name] = __import__('jax').numpy.asarray(drawn.astype(out[name].dtype))
    for name, factor in factors.items():
        out[name] = (out[name] * factor).astype(out[name].dtype)
    return out
```

```python
from contextlib import ExitStack

import concourse.bass as bass
from concourse import mybir

F32 = mybir.dt.float32
I32 = mybir.dt.int32
ALU = mybir.AluOpType
ACT = mybir.ActivationFunctionType

P = 128
D = 1024
KD = D // P
T = 1024
NREQ, TQ = 8, 8
PAST = 1024
PAGE = 128
NPAGE = PAST // PAGE
R = T + NREQ * TQ
NT = (R + P - 1) // P
RP = NT * P
NTP = T // P
HD = 64
NG, NKVH = 4, 2
FW = 512
CMP_N = (T - 32) // 16 + 1
WINDOW = 512
SEL = 64
DFF = 2816
NFF = DFF // P
PLE = 256
ALPHA = 2.0 ** 0.25
EPS = 1e-5
SCALE = HD ** -0.5
NEG = -1.0e30
FLOOR = 1.0e29
TINY = 1e-30
C_NQ, C_KV, C_FQ, C_FK = 0, 512, 1304, 1816
C_GA, C_GB = 2848, 3872
W_A, W_B, W_C, W_D, W_E = 0, 512, 792, 1304, 1816
W_N = 1824
DIST0 = PAST + TQ - 1
NDIST = 1160
BLOCKS = ((0, 363), (363, 363), (726, R - 726))
FFN_BLOCKS = ((0, 480), (480, 480), (960, R - 960))
QUERY_BLOCKS, QUERY_N = 4, R // 4
CMP, SLC, WIN, FOX = 0, 1, 2, 3


def split(w, n=512):
    return [(s, min(n, w - s)) for s in range(0, w, n)]


class Core:

    def __init__(self, nc, dram, ctx):
        self.nc, self.dram, self.ctx, self.live = nc, dram, ctx, []
        self.ps = ctx.enter_context(nc.psum_tensor("ps", [P, 8, 512], F32))
        self.bank = self.ps[:].rearrange("p b n -> p (b n)")

    def sems(self, *names):
        new = [self.nc.alloc_semaphore(name=n) for n in names]
        self.live += new
        return new

    def recycle(self):
        self.nc.clear_and_free_semaphores(self.live)
        self.nc.all_engine_barrier()
        self.live = []

    def scratch(self, name, shape):
        return self.nc.dram_tensor(name, shape, F32, kind="Internal").ap()


def project_rows(k, keep, io):
    nc, ps, bank = k.nc, k.ps, k.bank
    with ExitStack() as local:
        def sb(name, shape):
            return local.enter_context(nc.sbuf_tensor(name, shape, F32))

        w_rows = sb("w_rows", [P, KD, W_N])
        x_rows = sb("x_rows", [P, D])
        x_tile = sb("x_tile", [P, KD, P])
        kv4 = sb("kv4", [P, 512])
        win_gate = sb("win_gate", [P, 280])
        fk = sb("fk_rows", [P, FW])
        weights_in = k.sems("w_kv4_in", "w_win_in", "w_fk_in", "w_fv_in")
        (const_in, x_in, x_free, x_turned, turned_a, turned_b, xT_stored, kv4_ready, win_ready,
         fk_ready, fv_ready, ff_ready, kv4_staged, win_staged, fk_staged, fv_staged, ff_staged, pool_copied,
         rows_stored, stage_free, fk_turned, fk_saved, keys_turned, keys_saved) = k.sems(
            "const_in", "x_in", "x_free", "x_turned", "turned_a", "turned_b", "xT_stored",
            "kv4_ready", "win_ready", "fk_ready", "fv_ready", "ff_ready", "kv4_staged", "win_staged",
            "fk_staged", "fv_staged", "ff_staged", "pool_copied", "rows_stored", "stage_free", "fk_turned",
            "fk_saved", "keys_turned", "keys_saved")
        w_in = io["w_in"][0].rearrange("(k p) f -> p k f", p=P)
        block = local.enter_context(nc.Block())

        @block.sync
        def _(sp):
            sp.dma_start(keep.ident[:], io["c_ident"]).then_inc(const_in, 16)
            sp.dma_start(x_rows[:], io["x_all"][0:P, :]).then_inc(x_in, 16)
            for n, (a, b, c) in enumerate(((W_A, W_B, C_KV), (W_B, W_C, C_KV + W_B), (W_C, W_D, C_FK),
                                           (W_D, W_N, C_FK + FW))):
                sp.dma_start(w_rows[:, :, a:b], w_in[:, :, c:c + b - a]).then_inc(weights_in[n], 16)
            with sp.Fori(0, NT) as i:
                sp.wait_ge(x_turned, 2 * i + 2)
                sp.dma_start(x_rows[:], io["x_all"][bass.ds((i + 1) * P, P), :]).then_inc(x_in, 16)
                rows = bass.ds(i * P, P)
                sp.wait_ge(kv4_staged, i + 1)
                sp.dma_start(io["o_nsa_kv"][rows, :], kv4[:]).then_inc(rows_stored, 16)
                sp.wait_ge(win_staged, i + 1)
                sp.dma_start(io["o_win_rows"][rows, :], win_gate[:, 0:256]).then_inc(rows_stored, 16)
                sp.wait_ge(fk_staged, i + 1)
                sp.dma_start(io["o_fox_kv"][rows, 0:FW], fk[:]).then_inc(rows_stored, 16)
                sp.wait_ge(fv_staged, i + 1)
                sp.dma_start(io["o_fox_kv"][rows, FW:2 * FW],
                             keep.fv[:, bass.ds(i, 1), :].rearrange("p o f -> p (o f)")).then_inc(rows_stored, 16)
            sp.wait_ge(rows_stored, 64 * NT)
            sp.wait_ge(x_in, 16 * (NT + 1))

        @block.tensor
        def _(pe):
            pe.wait_ge(const_in, 16)
            with pe.Fori(0, NT) as i:
                pe.wait_ge(x_in, 16 * i + 16)
                for c in range(KD):
                    mm = pe.transpose(ps[:, c // 4, (c % 4) * P:(c % 4 + 1) * P],
                                      x_rows[:, c * P:(c + 1) * P], keep.ident[:])
                    if c % 4 == 3:
                        mm.then_inc(x_turned, 1)
                pe.wait_ge(turned_a, i + 1)
                pe.wait_ge(turned_b, i + 1)
                for n, (a, b, sem) in enumerate(((W_A, W_B, kv4_ready), (W_B, W_C, win_ready),
                                                 (W_C, W_D, fk_ready), (W_D, W_E, fv_ready),
                                                 (W_E, W_N, ff_ready))):
                    if n < 4:
                        pe.wait_ge(weights_in[n], 16)
                    for c in range(KD):
                        mm = pe.matmul(ps[:, 2 + n, 0:b - a], x_tile[:, c, :], w_rows[:, c, a:b],
                                       start=(c == 0), stop=(c == KD - 1))
                    mm.then_inc(sem, 1)
                pe.wait_ge(fk_staged, i + 1)
                for c in range(4):
                    mm = pe.transpose(ps[:, 7, c * P:(c + 1) * P], fk[:, c * P:(c + 1) * P], keep.ident[:])
                mm.then_inc(fk_turned, 1)
                pe.wait_ge(kv4_staged, i + 1)
                pe.wait_ge(win_staged, i + 1)
                pe.transpose(ps[:, 0, 0:P], kv4[:, 256:384], keep.ident[:])
                pe.transpose(ps[:, 0, P:2 * P], win_gate[:, 0:P], keep.ident[:]).then_inc(keys_turned, 1)
                pe.wait_ge(keys_saved, i + 1)
                pe.wait_ge(fk_saved, i + 1)

        @block.scalar
        def _(act):
            with act.Fori(0, NT) as i:
                act.wait_ge(x_turned, 2 * i + 1)
                act.wait_ge(xT_stored, i + 1)
                nc.scalar.copy(x_tile[:, 0:4, :], ps[:, 0, :].rearrange("p (c n) -> p c n", c=4)).then_inc(turned_a, 1)
                act.wait_ge(stage_free, i + 1)
                act.wait_ge(kv4_ready, i + 1)
                nc.scalar.copy(kv4[:], ps[:, 2, :]).then_inc(kv4_staged, 1)
                act.wait_ge(win_ready, i + 1)
                nc.scalar.copy(win_gate[:], ps[:, 3, 0:280]).then_inc(win_staged, 1)
                act.wait_ge(fk_turned, i + 1)
                nc.scalar.copy(keep.fkT[:, :, bass.ds(i * P, P)],
                               ps[:, 7, :].rearrange("p (c n) -> p c n", c=4)).then_inc(fk_saved, 1)

        @block.vector
        def _(dve):
            with dve.Fori(0, NT) as i:
                dve.wait_ge(x_turned, 2 * i + 2)
                dve.wait_ge(xT_stored, i + 1)
                nc.vector.tensor_copy(x_tile[:, 4:8, :],
                                      ps[:, 1, :].rearrange("p (c n) -> p c n", c=4)).then_inc(turned_b, 1)
                dve.wait_ge(stage_free, i + 1)
                dve.wait_ge(fk_ready, i + 1)
                nc.vector.tensor_copy(fk[:], ps[:, 4, :]).then_inc(fk_staged, 1)
                dve.wait_ge(fv_ready, i + 1)
                nc.vector.tensor_copy(keep.fv[:, bass.ds(i, 1), :],
                                      ps[:, 5, :].rearrange("p (o n) -> p o n", o=1)).then_inc(fv_staged, 1)
                dve.wait_ge(ff_ready, i + 1)
                nc.vector.tensor_copy(keep.ff[:, bass.ds(i, 1), :],
                                      ps[:, 6, 0:8].rearrange("p (o n) -> p o n", o=1)).then_inc(ff_staged, 1)
                dve.wait_ge(keys_turned, i + 1)
                nc.vector.tensor_copy(keep.keyT[:, :, bass.ds(i * P, P)],
                                      ps[:, 0, 0:2 * P].rearrange("p (c n) -> p c n", c=2)).then_inc(keys_saved, 1)

        @block.gpsimd
        def _(pool):
            pool.sem_inc(xT_stored, 1)
            pool.sem_inc(stage_free, 1)
            with pool.Fori(0, NT) as i:
                pool.wait_ge(turned_a, i + 1)
                pool.wait_ge(turned_b, i + 1)
                nc.gpsimd.tensor_copy(keep.xT[:, :, bass.ds(i * P, P)], x_tile[:]).then_inc(xT_stored, 1)
                pool.wait_ge(kv4_staged, i + 1)
                nc.gpsimd.tensor_copy(keep.v_slc[:, bass.ds(i, 1), :],
                                      kv4[:, 384:512].rearrange("p (o n) -> p o n", o=1)).then_inc(pool_copied, 1)
                pool.wait_ge(win_staged, i + 1)
                nc.gpsimd.tensor_copy(keep.v_win[:, bass.ds(i, 1), :],
                                      win_gate[:, P:2 * P].rearrange("p (o n) -> p o n", o=1)).then_inc(pool_copied, 1)
                nc.gpsimd.tensor_copy(keep.gates[:, bass.ds(i, 1), :],
                                      win_gate[:, 256:280].rearrange("p (o n) -> p o n", o=1)).then_inc(pool_copied, 1)
                pool.wait_ge(pool_copied, 3 * i + 3)
                pool.wait_ge(rows_stored, 64 * i + 64)
                pool.sem_inc(stage_free, 1)


def bias_tile(io, h, masked, first, rows, width):
    row = io["bias_rows"][h if isinstance(h, int) else bass.ds(h, 1)]
    return bass.AP(row.tensor, row.offset + (NDIST if masked else 0) + DIST0 + first, [[2 * NDIST - 1, rows], [1, width]])


def forget_and_bias(k, keep, io):
    nc, ps, bank = k.nc, k.ps, k.bank
    with ExitStack() as local:
        def sb(name, shape):
            return local.enter_context(nc.sbuf_tensor(name, shape, F32))

        bf = sb("bf", [P, 8])
        z, neg_abs, e, ln, w, logf = (sb(n, [P, NT, 8]) for n in ("z", "neg_abs", "e_abs", "ln_w", "w1p", "logf_rows"))
        ones = sb("ones_scan", [8, T])
        neg_logf = sb("neg_logf", [8, T])
        neg_c = sb("neg_c", [8, T])
        table = sb("table", [33, 8])
        onehot = sb("onehot", [33, 2 * NDIST])
        rev = sb("rev", [8, 2 * NDIST])
        (bias_in, z_done, act_done, dve_step, logf_done, logf_stored, logf_turned, logfT_done, neg_done, table_set,
         table_ready, rev_done, rev_stored, toeplitz_done, sums_done, sums_stored) = k.sems(
            "bias_in", "z_done", "act_done", "dve_step", "logf_done", "logf_stored", "logf_turned", "logfT_done",
            "neg_done", "table_set", "table_ready", "rev_done", "rev_stored", "toeplitz_done", "sums_done",
            "sums_stored")
        io["toeplitz_done"] = toeplitz_done
        block = local.enter_context(nc.Block())
        pieces = split(2 * NDIST, 464)

        @block.sync
        def _(sp):
            bf_row = io["b_forget"]
            sp.dma_start(bf[:], bass.AP(bf_row.tensor, 0, [[0, P], [1, 8]])).then_inc(bias_in, 16)
            sp.dma_start(table[0:32, :], io["rel_bias"]).then_inc(bias_in, 16)
            sp.dma_start(onehot[:], io["c_onehot"]).then_inc(bias_in, 16)
            sp.wait_ge(rev_done, len(pieces))
            sp.dma_start(io["rev"], rev[:]).then_inc(rev_stored, 16)
            sp.wait_ge(rev_stored, 16)
            for h in range(8):
                sp.dma_start(io["bias_rows"][h], bass.AP(io["rev"].tensor, h * 2 * NDIST, [[0, P], [1, 2 * NDIST]])).then_inc(toeplitz_done, 16)
            sp.wait_ge(logf_done, 1)
            sp.dma_start(io["o_logf"].rearrange("(i p) h -> p i h", p=P), logf[:]).then_inc(logf_stored, 16)
            sp.wait_ge(sums_done, 1)
            sp.dma_start(io["neg_sums"], neg_c[:]).then_inc(sums_stored, 16)
            sp.wait_ge(logf_stored, 16)
            sp.wait_ge(sums_stored, 16)

        @block.gpsimd
        def _(pool):
            nc.gpsimd.memset(table[32:33, :], NEG).then_inc(table_set, 1)
            nc.gpsimd.memset(ones[:], 1.0).then_inc(table_set, 1)

        @block.tensor
        def _(pe):
            pe.wait_ge(bias_in, 48)
            pe.wait_ge(table_set, 2)
            for n, (s, w_) in enumerate(pieces):
                pe.matmul(ps[0:8, 3 + n, 0:w_], table[:], onehot[:, s:s + w_], start=True, stop=True).then_inc(table_ready, 1)
            pe.wait_ge(logf_done, 1)
            for i in range(NT):
                mm = pe.transpose(ps[0:8, i // 4, (i % 4) * P:(i % 4 + 1) * P], logf[:, i, :], keep.ident[:])
            mm.then_inc(logf_turned, 1)

        @block.scalar
        def _(act):
            for n, (s, w_) in enumerate(pieces):
                act.wait_ge(table_ready, n + 1)
                nc.scalar.copy(rev[:, s:s + w_], ps[0:8, 3 + n, 0:w_]).then_inc(rev_done, 1)
            act.wait_ge(z_done, 3)
            nc.scalar.activation(e[:], neg_abs[:], ACT.Exp).then_inc(act_done, 1)
            act.wait_ge(act_done, 1)
            nc.scalar.activation(ln[:], e[:], ACT.Ln, bias=1.0).then_inc(act_done, 1)
            nc.scalar.activation(keep.gates[:], keep.gates[:], ACT.Sigmoid).then_inc(act_done, 1)
            act.wait_ge(logf_turned, 1)
            nc.scalar.copy(keep.logfT[:], bank[0:8, 0:RP]).then_inc(logfT_done, 1)

        @block.vector
        def _(dve):
            n = [0]

            def step(ins):
                n[0] += 1
                ins.then_inc(dve_step, 1)
                dve.wait_ge(dve_step, n[0])

            dve.wait_ge(bias_in, 48)
            nc.vector.tensor_tensor(z[:], keep.ff[:], bf[:].rearrange("p (o h) -> p o h", o=1).broadcast_to([P, NT, 8]),
                                    ALU.add).then_inc(z_done, 1)
            dve.wait_ge(z_done, 1)
            nc.vector.tensor_scalar(neg_abs[:], z[:], -1.0, None, ALU.mult).then_inc(z_done, 1)
            dve.wait_ge(z_done, 2)
            nc.vector.tensor_tensor(neg_abs[:], neg_abs[:], z[:], ALU.min).then_inc(z_done, 1)
            dve.wait_ge(act_done, 2)
            step(nc.vector.tensor_scalar(w[:], e[:], 1.0, None, ALU.add))
            step(nc.vector.tensor_scalar(w[:], w[:], 1.0, TINY, ALU.subtract, ALU.max))
            step(nc.vector.reciprocal(w[:], w[:]))
            step(nc.vector.tensor_tensor(w[:], w[:], e[:], ALU.mult))
            step(nc.vector.tensor_tensor(w[:], w[:], ln[:], ALU.mult))
            step(nc.vector.tensor_scalar(z[:], z[:], 0.0, None, ALU.min))
            nc.vector.tensor_tensor(logf[:], z[:], w[:], ALU.subtract).then_inc(logf_done, 1)
            dve.wait_ge(logfT_done, 1)
            dve.wait_ge(table_set, 2)
            step(nc.vector.tensor_scalar(neg_logf[:], keep.logfT[:, 0:T], -1.0, None, ALU.mult))
            nc.vector.tensor_tensor_scan(neg_c[:], ones[:], neg_logf[:], 0.0, ALU.mult, ALU.add).then_inc(sums_done, 1)


def project_queries(k, keep, io):
    nc, ps, bank = k.nc, k.ps, k.bank
    with ExitStack() as local:
        w_nsa = local.enter_context(nc.sbuf_tensor("w_nsa", [P, KD, P], F32))
        w_fox = local.enter_context(nc.sbuf_tensor("w_fox", [P, KD, P], F32))
        wn_in, wf_in, nsa_ready, fox_ready, nsa_saved, fox_saved = k.sems(
            "wn_in", "wf_in", "nsa_ready", "fox_ready", "nsa_saved", "fox_saved")
        w_in = io["w_in"][0].rearrange("(k p) f -> p k f", p=P)
        block = local.enter_context(nc.Block())

        @block.sync
        def _(sp):
            with sp.Fori(0, NG) as g:
                sp.wait_ge(nsa_saved, g + 1)
                for kvh in range(NKVH):
                    sp.dma_start(w_nsa[:, :, kvh * HD:(kvh + 1) * HD],
                                 w_in[:, :, bass.ds(C_NQ + kvh * NG * HD + g * HD, HD)]).then_inc(wn_in, 16)
                sp.wait_ge(fox_saved, g + 1)
                sp.dma_start(w_fox[:], w_in[:, :, bass.ds(C_FQ + g * P, P)]).then_inc(wf_in, 16)

        @block.tensor
        def _(pe):
            with pe.Fori(0, NG) as g:
                for base, w, w_there, per, ready, saved in ((0, w_nsa, wn_in, 32, nsa_ready, nsa_saved),
                                                            (QUERY_BLOCKS, w_fox, wf_in, 16, fox_ready, fox_saved)):
                    pe.wait_ge(w_there, per * g + per)
                    pe.wait_ge(saved, g + 1)
                    for b in range(QUERY_BLOCKS):
                        for c in range(KD):
                            mm = pe.matmul(ps[:, base + b, 0:QUERY_N], w[:, c, :], keep.xT[:, c, b * QUERY_N:(b + 1) * QUERY_N],
                                           start=(c == 0), stop=(c == KD - 1))
                    mm.then_inc(ready, 1)

        @block.scalar
        def _(act):
            act.sem_inc(nsa_saved, 1)
            with act.Fori(0, NG) as g:
                act.wait_ge(nsa_ready, g + 1)
                nc.scalar.activation(keep.qT[:, bass.ds(g, 1), :].rearrange("p o (b n) -> p (o b) n", b=QUERY_BLOCKS),
                                     ps[:, 0:QUERY_BLOCKS, 0:QUERY_N],
                                     ACT.Copy, scale=SCALE).then_inc(nsa_saved, 1)

        @block.vector
        def _(dve):
            dve.sem_inc(fox_saved, 1)
            with dve.Fori(0, NG) as g:
                dve.wait_ge(fox_ready, g + 1)
                nc.vector.tensor_scalar(keep.qfT[:, bass.ds(g, 1), :].rearrange("p o (b n) -> p (o b) n", b=QUERY_BLOCKS),
                                        ps[:, QUERY_BLOCKS:2 * QUERY_BLOCKS, 0:QUERY_N], SCALE, None, ALU.mult).then_inc(fox_saved, 1)


def load_compressor(eng, io, cw, there):
    for kv in range(2):
        eng.dma_start(cw.w1[:, kv], io["nsa_cmp_w1"][0, kv].rearrange("(l two) d k -> (two d) l k", two=2)).then_inc(there, 16)
        eng.dma_start(cw.w2[:, kv], io["nsa_cmp_w2"][0, kv]).then_inc(there, 16)
        eng.dma_start(cw.pe[:, kv], io["nsa_cmp_pe"][0, kv].rearrange("(l two) d -> (two d) l", two=2), allow_slow_non_contiguous=True).then_inc(there, 16)


COMPRESSOR_DMAS = 6


class Compressor:
    def __init__(self, sb, tag):
        self.w1 = sb("cmp_w1" + tag, [P, 2, 16, P])
        self.w2 = sb("cmp_w2" + tag, [P, 2, HD])
        self.pe = sb("cmp_pe" + tag, [P, 2, 16])
        self.bias = sb("cmp_bias" + tag, [P, 2])
        self.rawT = sb("cmp_rawT" + tag, [P, 4, 512])
        self.hid = sb("cmp_hid" + tag, [P, 2, 2, CMP_N])


def position_bias(pe, cw, out):
    for kv in range(2):
        for l in range(16):
            mm = pe.matmul(out[:, kv:kv + 1], cw.w1[:, kv, l, :], cw.pe[:, kv, l:l + 1], start=(l == 0), stop=(l == 15))
    return mm


def hidden_layer(pe, cw, out):
    for kv in range(2):
        for l in range(16):
            mm = pe.matmul(out[:, kv * 2 * CMP_N:(kv + 1) * 2 * CMP_N].rearrange("p (h n) -> p h n", h=2),
                           cw.w1[:, kv, l, :], cw.rawT[:, 2 * kv:2 * kv + 2, l:l + 8 * (CMP_N - 1) + 1:8],
                           start=(l == 0), stop=(l == 15))
    return mm


def compressed_kv(pe, cw, out):
    for h in range(2):
        pe.matmul(out[h * HD:(h + 1) * HD, 0:CMP_N], cw.w2[:, 0, :], cw.hid[:, 0, h, :], start=True, stop=True)
    for h in range(2):
        mm = pe.matmul(out[0:CMP_N, HD + h * HD:HD + (h + 1) * HD], cw.hid[:, 1, h, :], cw.w2[:, 1, :], start=True, stop=True)
    return mm


def compress_prompt(k, keep, io):
    nc, ps, bank = k.nc, k.ps, k.bank
    with ExitStack() as local:
        def sb(name, shape):
            return local.enter_context(nc.sbuf_tensor(name, shape, F32))

        cw = Compressor(sb, "_p")
        raw = sb("cmp_raw_p", [P, 4, 4, 2, HD])
        (cw_in, raw_in, pb_ready, pb_saved, raw_turned, rawT_a, rawT_b, hid_ready, hid_saved, kcvc_ready,
         kcvc_saved) = k.sems(
            "cw_in", "raw_in", "pb_ready", "pb_saved", "raw_turned", "rawT_a", "rawT_b", "hid_ready", "hid_saved",
            "kcvc_ready", "kcvc_saved")
        block = local.enter_context(nc.Block())

        @block.sync
        def _(sp):
            load_compressor(sp, io, cw, cw_in)
            src = io["o_nsa_kv"][0:T, 0:256].rearrange("(r q two) (c d) -> r two q c d", q=P, two=2, d=HD)
            for r in range(4):
                for par in range(2):
                    sp.dma_start(raw[:, r, :, par, :], src[r, par]).then_inc(raw_in, 16)

        @block.tensor
        def _(pe):
            pe.wait_ge(cw_in, 16 * COMPRESSOR_DMAS)
            position_bias(pe, cw, ps[:, 2, :]).then_inc(pb_ready, 1)
            pe.wait_ge(raw_in, 16 * 8)
            for c in range(4):
                if c >= 2:
                    pe.wait_ge((rawT_a, rawT_b)[c % 2], 1)
                for r in range(4):
                    mm = pe.transpose(ps[:, c % 2, r * P:(r + 1) * P], raw[:, r, c].rearrange("p t d -> p (t d)"), keep.ident[:])
                mm.then_inc(raw_turned, 1)
            pe.wait_ge(rawT_a, 2)
            pe.wait_ge(rawT_b, 2)
            hidden_layer(pe, cw, ps[:, 3, :]).then_inc(hid_ready, 1)
            pe.wait_ge(hid_saved, 2)
            compressed_kv(pe, cw, ps[:, 4, :]).then_inc(kcvc_ready, 1)

        @block.scalar
        def _(act):
            for c in (0, 2):
                act.wait_ge(raw_turned, c + 1)
                nc.scalar.copy(cw.rawT[:, c, :], ps[:, 0, :]).then_inc(rawT_a, 1)
            act.wait_ge(hid_ready, 1)
            act.wait_ge(pb_saved, 1)
            for kv in range(2):
                nc.scalar.activation(cw.hid[:, kv].rearrange("p h n -> p (h n)"),
                                     ps[:, 3, kv * 2 * CMP_N:(kv + 1) * 2 * CMP_N], ACT.Gelu_apprx_tanh,
                                     bias=cw.bias[:, kv:kv + 1]).then_inc(hid_saved, 1)

        @block.vector
        def _(dve):
            dve.wait_ge(pb_ready, 1)
            nc.vector.tensor_copy(cw.bias[:], ps[:, 2, 0:2]).then_inc(pb_saved, 1)
            for c in (1, 3):
                dve.wait_ge(raw_turned, c + 1)
                nc.vector.tensor_copy(cw.rawT[:, c, :], ps[:, 1, :]).then_inc(rawT_b, 1)
            dve.wait_ge(kcvc_ready, 1)
            nc.vector.tensor_copy(keep.kcT[:, 0:CMP_N], ps[:, 4, 0:CMP_N]).then_inc(kcvc_saved, 1)
            nc.vector.tensor_copy(keep.vc[0:CMP_N, :], ps[0:CMP_N, 4, HD:HD + P]).then_inc(kcvc_saved, 1)


class Unit:

    def __init__(self, n, i, half, branch):
        self.n, self.i, self.half, self.branch = n, i, half, branch
        self.group = 2 * i + half
        if branch == CMP:
            self.k0, self.width = 0, 8 * i + 7
        elif branch == WIN:
            t0 = max(0, i - WINDOW // P)
            self.k0, self.width = t0 * P, (i + 1 - t0) * P
        else:
            self.k0, self.width = 0, (i + 1) * P
        self.tiles = [(self.k0 // P + j, s, w) for j, (s, w) in enumerate(split(self.width, P))]


UNITS = [Unit(((i * 2 + half) * 4 + j), i, half, br)
         for i in range(NTP) for half in range(2) for j, br in enumerate((SLC, FOX, WIN, CMP))]
WIDE = [u for u in UNITS if len(u.tiles) > 4]
NU, NWIDE, NGROUP = len(UNITS), len(WIDE), 2 * NTP


def prompt_attention(k, keep, io):
    nc, ps, bank = k.nc, k.ps, k.bank
    with ExitStack() as local:
        def sb(name, shape):
            return local.enter_context(nc.sbuf_tensor(name, shape, F32))

        q_nsa, q_fox = sb("q_nsa", [P, 2, T]), sb("q_fox", [P, 2, T])
        gate = sb("gate", [P, NTP, 2, 4])
        bias_slc = sb("bias_slc_sb", [P, 2, T])
        bias_win = sb("bias_win_sb", [P, 2, WINDOW + P])
        bias_fox = sb("bias_fox_sb", [P, 2, T])
        diag_fox = sb("diag_fox", [P, 2, NTP, P])
        causal = sb("causal", [P, P])
        probs = sb("probs", [P, 3, T])
        probsT = sb("probsT", [P, 8, P])
        nmax = sb("nmax", [P, 4, 2])
        sums = sb("sums", [P, 4, 4])
        coef = sb("coef", [P, 4])
        out = sb("out_rows", [P, 2, 4, 2, HD])
        (mask_in, bias_in, zeroed, q_ready, gate_ready, scores_ready, half_max, logits_ready, probs_ready, turned0, turned1,
         probsT0, probsT1, pv_ready, scaled, coef_step, combined, comb_step, outT_ready, outT_saved, diag_ready, pe_passed, dve_passed, sp_passed, pool_passed) = k.sems(
            "mask_in", "head_bias_in", "q_zeroed", "q_ready", "gate_ready", "scores_ready", "half_max", "logits_ready", "probs_ready",
            "turned0", "turned1", "probsT0", "probsT1", "pv_ready", "scaled", "coef_step", "combined", "comb_step",
            "outT_ready", "outT_saved", "diag_ready", "pe_passed", "dve_passed",
            "sp_passed", "pool_passed")
        wide_no = {u.n: j for j, u in enumerate(WIDE)}
        DIAG0 = next(u.n for u in UNITS if u.branch == FOX)

        def scores_psum(u, s=0, w=None):
            base = (u.n % 2) * 1024
            return bank[:, base + s:base + s + (u.width if w is None else w)]

        block = local.enter_context(nc.Block())

        @block.sync
        def _(sp):
            sp.dma_start(causal[:], io["c_causal"]).then_inc(mask_in, 16)
            sp.wait_ge(io["toeplitz_done"], 16 * 8)
            with sp.Fori(0, NG) as g:
                for half in range(2):
                    sp.dma_start(bias_slc[:, half, :], bias_tile(io, half * NG + g, False, P - T, P, T)).then_inc(bias_in, 16)
                    sp.dma_start(bias_win[:, half, :], bias_tile(io, half * NG + g, True, -WINDOW, P, WINDOW + P)).then_inc(bias_in, 16)
                    row = io["neg_sums"][bass.ds(2 * g + half, 1), :]
                    sp.dma_start(bias_fox[:, half, :], bass.AP(row.tensor, row.offset, [[0, P], [1, T]])).then_inc(bias_in, 16)
                sp.wait_ge(logits_ready, NU * g + NU)
                sp.sem_inc(sp_passed, 1)

        @block.gpsimd
        def _(pool):
            def refill(turn, i):
                for half in range(2):
                    rows = slice(half * HD, (half + 1) * HD)
                    for q, kept in ((q_nsa, keep.qT), (q_fox, keep.qfT)):
                        nc.gpsimd.tensor_copy(q[rows, half, i * P:(i + 1) * P],
                                              kept[rows, bass.ds(turn, 1), i * P:(i + 1) * P].rearrange("p o n -> p (o n)")).then_inc(q_ready, 1)
                    pool.wait_ge(q_ready, 4 * (NTP * turn + i) + 2 * half + 2)
                    pool.sem_inc(pool_passed, 1)

            def set_gates(turn):
                for half in range(2):
                    nc.gpsimd.tensor_copy(gate[:, :, half, 0:3], keep.gates[:, 0:NTP, bass.ds(half * 12 + turn * 3, 3)]).then_inc(gate_ready, 1)

            def one_turn(g, more):
                pool.wait_ge(bias_in, 96 * g + 96)
                for half in range(2):
                    nc.gpsimd.tensor_tensor(diag_fox[:, half], bias_fox[:, half, :].rearrange("p (i n) -> p i n", i=NTP),
                                            causal[:].rearrange("p (o n) -> p o n", o=1).broadcast_to([P, NTP, P]),
                                            ALU.add).then_inc(diag_ready, 1)
                for n in range(NGROUP):
                    i, half = n // 2, n % 2
                    o = out[:, i % 2, :, half, :]
                    pool.wait_ge(scaled, NGROUP * g + n + 1)
                    nc.gpsimd.tensor_tensor(o[:, CMP], o[:, CMP], o[:, SLC], ALU.add).then_inc(comb_step, 1)
                    pool.wait_ge(comb_step, NGROUP * g + n + 2)
                    nc.gpsimd.tensor_tensor(o[:, CMP], o[:, CMP], o[:, WIN], ALU.add).then_inc(combined, 1)
                    if more and half:
                        if i == 0:
                            pool.wait_ge(q_ready, 4 * NTP * (g + 1))
                            pool.sem_inc(pool_passed, 1)
                        refill(g + 1, i)
                if more:
                    set_gates(g + 1)

            nc.gpsimd.memset(gate[:], 1.0).then_inc(comb_step, 1)
            pool.wait_ge(comb_step, 1)
            set_gates(0)
            pool.wait_ge(mask_in, 16)
            with pool.Fori(0, NG - 1) as g:
                one_turn(g, True)
            one_turn(NG - 1, False)

        @block.tensor
        def _(pe):
            def scores(g, u):
                if u.n % 8 == 0:
                    pe.wait_ge(q_ready, 4 * (NTP * g + u.i) + 4)
                    pe.sem_inc(pe_passed, 1)
                q = (q_fox if u.branch == FOX else q_nsa)[:, u.half, u.i * P:(u.i + 1) * P]
                for s, w in split(u.width):
                    cols = slice(u.k0 + s, u.k0 + s + w)
                    if u.branch == FOX:
                        keys = keep.fkT[:, bass.ds(g, 1), cols].rearrange("p o n -> p (o n)")
                    else:
                        keys = {CMP: keep.kcT[:], SLC: keep.keyT[:, 0], WIN: keep.keyT[:, 1]}[u.branch][:, cols]
                    mm = pe.matmul(scores_psum(u, s, w), q, keys, start=True, stop=True)
                mm.then_inc(scores_ready, 1)

            def out_turned(g, i):
                pe.wait_ge(combined, NGROUP * g + 2 * i + 2)
                for j, br in enumerate((CMP, FOX)):
                    mm = pe.transpose(ps[:, 5, j * P:(j + 1) * P],
                                      out[:, i % 2, br].rearrange("p h d -> p (h d)"), keep.ident[:])
                mm.then_inc(outT_ready, 1)

            pe.wait_ge(q_ready, 4 * NTP)
            with pe.Fori(0, NG) as g:
                scores(g, UNITS[0])
                scores(g, UNITS[1])
                for u in UNITS:
                    n = NU * g + u.n
                    if u.n in wide_no and u.n % 8 == 4:
                        pe.wait_ge(outT_saved, NTP * g + u.i)
                    pe.wait_ge(probs_ready, n + 1)
                    pe.sem_inc(pe_passed, 1)
                    for j, (kt, s, w) in enumerate(u.tiles):
                        mm = pe.transpose(ps[0:w, 4 + j // 4, (j % 4) * P:(j % 4 + 1) * P],
                                          probs[:, u.n % 3, s:s + w], keep.ident[:])
                        if j == min(3, len(u.tiles) - 1):
                            mm.then_inc(turned0, 1)
                        elif j == len(u.tiles) - 1:
                            mm.then_inc(turned1, 1)
                    if u.n + 2 < NU:
                        scores(g, UNITS[u.n + 2])
                    pe.wait_ge(probsT0, n + 1)
                    if u.n in wide_no:
                        pe.wait_ge(probsT1, NWIDE * g + wide_no[u.n] + 1)
                    if u.n % 4 == 0 and u.group >= 2:
                        pe.wait_ge(scaled, NGROUP * g + u.group - 1)
                    o = ps[:, 6 + u.half, u.branch * P:(u.branch + 1) * P]
                    for j, (kt, s, w) in enumerate(u.tiles):
                        if u.branch == CMP:
                            v = keep.vc[0:w, :]
                        elif u.branch == FOX:
                            v = keep.fv[:, kt, bass.ds(g * P, P)]
                        else:
                            v = (keep.v_slc if u.branch == SLC else keep.v_win)[:, kt, :]
                        mm = pe.matmul(o, probsT[0:w, j, :], v, start=(j == 0), stop=(j == len(u.tiles) - 1))
                    mm.then_inc(pv_ready, 1)
                    if u.n % 8 == 2 and u.i >= 1:
                        out_turned(g, u.i - 1)
                out_turned(g, NTP - 1)
                pe.wait_ge(outT_saved, NTP * g + NTP)

        @block.vector
        def _(dve):
            def logits(g, u):
                dve.wait_ge(scores_ready, NU * g + u.n + 1)
                dve.sem_inc(dve_passed, 1)
                dst = probs[:, u.n % 3, 0:u.width]
                if u.branch == FOX:
                    first = u.width - P
                    if first:
                        nc.vector.tensor_tensor_reduce(dst[:, 0:first], scores_psum(u, 0, first), bias_fox[:, u.half, 0:first],
                                                       -1.0, FLOOR, ALU.add, ALU.min, nmax[:, u.n % 4, 1:2]).then_inc(half_max, 1)
                        dve.wait_ge(half_max, (NTP - 1) * 2 * g + (u.i - 1) * 2 + u.half + 1)
                        dve.sem_inc(dve_passed, 1)
                    nc.vector.tensor_tensor_reduce(dst[:, first:], scores_psum(u, first, P), diag_fox[:, u.half, u.i, :],
                                                   -1.0, nmax[:, u.n % 4, 1:2] if first else FLOOR,
                                                   ALU.add, ALU.min, nmax[:, u.n % 4, 0:1]).then_inc(logits_ready, 1)
                    return
                if u.branch == SLC:
                    bias = bias_slc[:, u.half, T - u.width:T]
                elif u.branch == WIN:
                    bias = bias_win[:, u.half, WINDOW + P - u.width:WINDOW + P]
                else:
                    first = T - P + 31 - u.i * P
                    bias = bias_slc[:, u.half, first:first + 16 * (u.width - 1) + 1:16]
                nc.vector.tensor_tensor_reduce(dst, scores_psum(u), bias, -1.0, FLOOR, ALU.add, ALU.min,
                                               nmax[:, u.n % 4, 0:1]).then_inc(logits_ready, 1)

            def scale(g, n):
                i, half = n // 2, n % 2
                dve.wait_ge(pv_ready, NU * g + 4 * n + 4)
                base = 3 * NGROUP * g + 3 * n
                nc.vector.tensor_scalar(coef[:], sums[:, n % 4, :], TINY, None, ALU.max).then_inc(coef_step, 1)
                dve.wait_ge(coef_step, base + 1)
                nc.vector.reciprocal(coef[:], coef[:]).then_inc(coef_step, 1)
                dve.wait_ge(coef_step, base + 2)
                nc.vector.tensor_tensor(coef[:], coef[:], gate[:, i, half, :], ALU.mult).then_inc(coef_step, 1)
                dve.wait_ge(coef_step, base + 3)
                if i >= 2:
                    dve.wait_ge(outT_ready, NTP * g + i - 1)
                nc.vector.tensor_tensor(out[:, i % 2, :, half, :],
                                        ps[:, 6 + half, :].rearrange("p (b h d) -> p b h d", b=4, h=2)[:, :, half, :],
                                        coef[:].rearrange("p (b o) -> p b o", o=1).broadcast_to([P, 4, HD]),
                                        ALU.mult).then_inc(scaled, 1)

            for q in (q_fox, q_nsa):
                nc.vector.memset(q[:], 0.0).then_inc(zeroed, 1)
            dve.wait_ge(zeroed, 2)
            for half in range(2):
                rows = slice(half * HD, (half + 1) * HD)
                nc.vector.tensor_copy(q_nsa[rows, half, :], keep.qT[rows, 0, 0:T]).then_inc(q_ready, NTP)
            with dve.Fori(0, NG) as g:
                dve.wait_ge(bias_in, 96 * g + 96)
                dve.wait_ge(gate_ready, 2 * g + 2)
                dve.wait_ge(diag_ready, 2 * g + 2)
                logits(g, UNITS[0])
                logits(g, UNITS[1])
                for u in UNITS:
                    n = NU * g + u.n
                    dve.wait_ge(turned0, n + 1)
                    w, m = u.tiles[0][2], min(4, len(u.tiles))
                    nc.vector.tensor_copy(probsT[0:w, 0:m, :], ps[0:w, 4, 0:m * P].rearrange("p (j q) -> p j q", j=m)).then_inc(probsT0, 1)
                    if u.n + 2 < NU:
                        logits(g, UNITS[u.n + 2])
                    if u.n % 4 == 0 and u.n:
                        scale(g, u.group - 1)
                scale(g, NGROUP - 1)

        @block.scalar
        def _(act):
            def exps(g, u):
                act.wait_ge(logits_ready, NU * g + u.n + 1)
                p_ = probs[:, u.n % 3, 0:u.width]
                nc.scalar.activation(p_, p_, ACT.Exp, bias=nmax[:, u.n % 4, 0:1], scale=-1.0,
                                     accum_out=sums[:, u.group % 4, u.branch:u.branch + 1]).then_inc(probs_ready, 1)

            def save_out(g, i):
                act.wait_ge(outT_ready, NTP * g + i + 1)
                nc.scalar.copy(keep.qT[:, bass.ds(g, 1), i * P:(i + 1) * P].rearrange("p o n -> p (o n)"), ps[:, 5, 0:P])
                nc.scalar.copy(keep.qfT[:, bass.ds(g, 1), i * P:(i + 1) * P].rearrange("p o n -> p (o n)"),
                               ps[:, 5, P:2 * P]).then_inc(outT_saved, 1)

            act.wait_ge(zeroed, 1)
            for half in range(2):
                rows = slice(half * HD, (half + 1) * HD)
                nc.scalar.copy(q_fox[rows, half, :], keep.qfT[rows, 0, 0:T]).then_inc(q_ready, NTP)
            with act.Fori(0, NG) as g:
                exps(g, UNITS[0])
                exps(g, UNITS[1])
                for u in UNITS:
                    if u.n in wide_no:
                        act.wait_ge(turned1, NWIDE * g + wide_no[u.n] + 1)
                        m = len(u.tiles) - 4
                        nc.scalar.copy(probsT[:, 4:4 + m, :], ps[:, 5, 0:m * P].rearrange("p (j q) -> p j q", j=m)).then_inc(probsT1, 1)
                    if u.n + 2 < NU:
                        exps(g, UNITS[u.n + 2])
                    if u.n % 8 == 2 and u.i >= 1:
                        save_out(g, u.i - 1)
                save_out(g, NTP - 1)


def load_pages(sp, io, b, cache_pages, ids):
    return [sp.value_load(ids[0:1, bass.ds(b * NPAGE + p, 1)], min_val=0, max_val=cache_pages - 1) for p in range(NPAGE)]


def request_attention(k, keep, io):
    nc, ps, bank = k.nc, k.ps, k.bank
    KEYS = PAST + TQ
    with ExitStack() as local:
        def sb(name, shape, dt=F32):
            return local.enter_context(nc.sbuf_tensor(name, shape, dt))

        cw = Compressor(sb, "_r")
        ids = sb("page_ids", [1, NREQ * NPAGE], I32)
        k_fox, v_fox = sb("k_pages", [P, NPAGE, FW]), sb("v_pages", [P, NPAGE, FW])
        kv_slc = sb("slc_pages", [P, NPAGE, 2 * P])
        raw = sb("cmp_raw_r", [P, 4, 4, 2, HD])
        kv_win = sb("win_buf", [P, 4, 2 * P])
        logf_pages = sb("logf_pages", [P, NPAGE, 8])
        new_fox, new_nsa, new_win = sb("new_fox", [TQ, 2 * FW]), sb("new_nsa", [TQ, 512]), sb("new_win", [TQ, 2 * P])
        k_foxT, k_slcT, k_winT = sb("k_foxT", [P, 4, KEYS]), sb("k_slcT", [P, KEYS]), sb("k_winT", [P, WINDOW + TQ])
        q_nsa, q_fox = sb("q_nsa_r", [P, 64]), sb("q_fox_r", [P, 4 * 80])
        neg_c = sb("neg_c_r", [8, KEYS])
        one, zero = sb("one", [8, 1]), sb("zero", [64, 1])
        kcT, vc = sb("kcT_r", [P, 64]), sb("vc_r", [64, P])
        bias_slc, bias_win = sb("bias_slc_r", [64, KEYS]), sb("bias_win_r", [64, WINDOW + TQ])
        new_mask = sb("new_mask", [64, TQ])
        p_fox, p_win = sb("p_fox", [64, KEYS]), sb("p_win", [64, WINDOW + TQ])
        p_slc = p_fox
        p_cmp, p_cmp_n, p_cmp_g = sb("p_cmp", [64, 64]), sb("p_cmp_n", [64, 64]), sb("p_cmp_g", [64, 64])
        pT_fox, pT_win = sb("pT_fox", [P, 9, 64]), sb("pT_win", [P, 5, 64])
        pT_slc = pT_fox
        pT_cmp, pT_gated = sb("pT_cmp", [64, 64]), sb("pT_gated", [64, 64])
        overlap, same, spread = sb("overlap", [CMP_N, 17]), sb("same", [64, 64]), sb("spread", [8, 64])
        block_no, block_mask = sb("block_no", [64, 16]), sb("block_mask", [64, 16])
        importance, pick = sb("importance", [64, 17]), sb("pick", [64, 16])
        gates = sb("gates_r", [64, NREQ, 3])
        nmax, sums, coef = sb("nmax_r", [64, 4]), sb("sums_r", [64, 4]), sb("coef_r", [64, 4])
        (gate_rows_out, ready_in, cw_in, win_copied, early_in, late_in, queries_ready, neg_c_ready, dve_step, turned,
         act_saved, dve_saved, hid_ready, hid_saved, kcvc_ready, kcvc_saved, scores_ready, logits_ready, probs_ready,
         scaled, imp_ready, imp_saved, out_ready, out_saved, pb_ready, pb_saved, set_ready, dve_noted, pe_noted) = k.sems(
            "gate_rows_out", "ready_in", "cw_in_r", "win_copied", "early_in", "late_in", "queries_ready",
            "neg_c_ready", "dve_step_r", "turned_r", "act_saved", "dve_saved", "hid_ready_r", "hid_saved_r",
            "kcvc_ready_r", "kcvc_saved_r", "scores_ready_r", "logits_ready_r", "probs_ready_r", "scaled_r",
            "imp_ready", "imp_saved", "out_ready", "out_saved", "pb_ready_r", "pb_saved_r", "set_ready",
            "dve_noted", "pe_noted")
        TURNS = ["logf0", "logf1"] + [f"fox{p}" for p in range(8)] + [f"raw{c}" for c in range(4)] + [
            "fox_new", "slc0", "slc1", "slc_new", "win", "win_new", "p_fox", "p_fox_new", "p_cmp", "p_win",
            "p_gated", "p_win_new", "p_slc", "p_slc_new"]
        NTURN = len(TURNS)
        EARLY = TURNS.index("raw3") + 1
        F, W, C, S = 0, 1, 2, 3
        EARLY_DMAS, LATE_DMAS = 4 * NPAGE, 2 * NPAGE + 4
        row0 = T
        cache_pages = io["cache_fox_kv"].shape[1]
        block = local.enter_context(nc.Block())

        @block.sync
        def _(sp):
            sp.dma_start(ids[:], bass.AP(io["page_table"].tensor, 0, [[NREQ * NPAGE, 1], [1, NREQ * NPAGE]])).then_inc(gate_rows_out, 16)
            sp.dma_start(io["gate_rows"], keep.gates[0:64, NTP, :]).then_inc(gate_rows_out, 16)
            load_compressor(sp, io, cw, cw_in)
            sp.dma_start(io["o_win_sample"][:, 0:WINDOW - TQ, :],
                         io["state_nsa_win"][0].rearrange("b t k h d -> b t (k h d)")[:, TQ:WINDOW, :]).then_inc(win_copied, 16)
            sp.dma_start(io["o_win_sample"][:, WINDOW - TQ:WINDOW, :],
                         io["o_win_rows"][row0:R, :].rearrange("(b t) c -> b t c", t=TQ)).then_inc(win_copied, 16)
            for name, dst in (("c_newmask", new_mask), ("c_overlap", overlap), ("c_same", same), ("c_spread", spread),
                              ("c_block", block_no)):
                sp.dma_start(dst[:], io[name]).then_inc(ready_in, 16)
            for h in range(8):
                for w, dst, first, n in ((0, bias_slc, 0, KEYS), (1, bias_win, PAST - WINDOW, WINDOW + TQ)):
                    sp.dma_start(dst[h * 8:(h + 1) * 8, :], bias_tile(io, h, w, first - PAST, TQ, n)).then_inc(ready_in, 16)
            sp.wait_ge(gate_rows_out, 32)
            for h in range(8):
                sp.dma_start(gates[h * 8:(h + 1) * 8, :, :],
                             bass.AP(io["gate_rows"].tensor, h * 3, [[24, TQ], [24 * TQ, NREQ], [1, 3]])).then_inc(ready_in, 16)
            with sp.Fori(0, NREQ) as b:
                pages = load_pages(sp, io, b, cache_pages, ids)
                sp.wait_ge(turned, NTURN * b + EARLY)
                for p in range(NPAGE):
                    fox = io["cache_fox_kv"][0, bass.ds(pages[p], 1)].rearrange("o t k h d -> (o t) k (h d)")
                    nsa = io["cache_nsa_kv"][0, bass.ds(pages[p], 1)].rearrange("o t k h d -> (o t) (k h d)")
                    sp.dma_start(logf_pages[:, p, :], io["cache_fox_logf"][0, bass.ds(pages[p], 1)].rearrange("o t h -> (o t) h")).then_inc(early_in, 16)
                    sp.dma_start(k_fox[:, p, :], fox[:, 0, :]).then_inc(early_in, 16)
                    pairs = nsa[:, 0:256].rearrange("(q two) (c d) -> two q c d", two=2, d=HD)
                    for par in range(2):
                        sp.dma_start(raw[(p % 2) * 64:(p % 2) * 64 + 64, p // 2, :, par, :], pairs[par]).then_inc(early_in, 16)
                sp.wait_ge(out_ready, 2 * b + 2)
                rows = bass.ds(row0 + b * TQ, TQ)
                sp.dma_start(new_fox[:], io["o_fox_kv"][rows, :]).then_inc(late_in, 16)
                sp.dma_start(new_nsa[:], io["o_nsa_kv"][rows, :]).then_inc(late_in, 16)
                sp.dma_start(new_win[:], io["o_win_rows"][rows, :]).then_inc(late_in, 16)
                sp.dma_start(kv_win[:], io["state_nsa_win"][0, bass.ds(b, 1)].rearrange("o (j p) k h d -> p (o j) (k h d)", p=P)).then_inc(late_in, 16)
                for p in range(NPAGE):
                    fox = io["cache_fox_kv"][0, bass.ds(pages[p], 1)].rearrange("o t k h d -> (o t) k (h d)")
                    nsa = io["cache_nsa_kv"][0, bass.ds(pages[p], 1)].rearrange("o t k h d -> (o t) (k h d)")
                    sp.dma_start(kv_slc[:, p, :], nsa[:, 256:512]).then_inc(late_in, 16)
                    sp.dma_start(v_fox[:, p, :], fox[:, 1, :]).then_inc(late_in, 16)
            sp.wait_ge(win_copied, 32)

        @block.gpsimd
        def _(pool):
            for t in (q_nsa, q_fox):
                nc.gpsimd.memset(t[:], 0.0).then_inc(set_ready, 1)
            nc.gpsimd.memset(one[:], 1.0).then_inc(set_ready, 1)
            nc.gpsimd.memset(zero[:], 0.0).then_inc(set_ready, 1)

        @block.tensor
        def _(pe):
            pe.sem_inc(turned, NTURN)
            pe.sem_inc(out_ready, 2)
            pe.wait_ge(cw_in, 16 * COMPRESSOR_DMAS)
            position_bias(pe, cw, ps[:, 7, :]).then_inc(pb_ready, 1)
            pe.wait_ge(pb_saved, 1)
            pe.wait_ge(ready_in, 16 * (5 + 16 + 8))
            pe.wait_ge(set_ready, 4)
            with pe.Fori(0, NREQ) as b:
                state = {"n": 0}

                def saved(n):
                    pe.wait_ge((act_saved, dve_saved)[n % 2], (NTURN // 2) * b + n // 2 + 1)

                def turn(name, items):
                    n = state["n"]
                    assert TURNS[n] == name
                    if n >= 2:
                        saved(n - 2)
                        pe.sem_inc(pe_noted, 1)
                    for rows, cols, src in items:
                        kk = src.shape[0]
                        mm = pe.transpose(ps[0:rows, n % 2, cols[0]:cols[1]], src, keep.ident[0:kk, 0:kk])
                    mm.then_inc(turned, 1)
                    state["n"] += 1

                pe.wait_ge(early_in, 16 * EARLY_DMAS * (b + 1))
                for half in range(2):
                    turn(f"logf{half}", [(8, (j * P, (j + 1) * P), logf_pages[:, 4 * half + j, :]) for j in range(4)])
                for p in range(NPAGE):
                    turn(f"fox{p}", [(P, (c * P, (c + 1) * P), k_fox[:, p, c * P:(c + 1) * P]) for c in range(4)])
                for c in range(4):
                    turn(f"raw{c}", [(P, (r * P, (r + 1) * P), raw[:, r, c].rearrange("p t d -> p (t d)")) for r in range(4)])
                saved(EARLY - 2)
                saved(EARLY - 1)
                pe.wait_ge(out_saved, 2 * b + 2)
                hidden_layer(pe, cw, ps[:, 5, :]).then_inc(hid_ready, 1)
                pe.wait_ge(late_in, 16 * LATE_DMAS * (b + 1))
                turn("fox_new", [(P, (c * TQ, (c + 1) * TQ), new_fox[:, c * P:(c + 1) * P]) for c in range(4)])
                saved(EARLY)
                pe.wait_ge(queries_ready, 2 * b + 2)
                pe.wait_ge(neg_c_ready, b + 1)
                for s, w in split(KEYS):
                    for c in range(4):
                        pe.matmul(ps[0:64, 2 + s // 512, 0:w], q_fox[:, c * 64:(c + 1) * 64], k_foxT[:, c, s:s + w],
                                  start=(c == 0), stop=False)
                    mm = pe.matmul(ps[0:64, 2 + s // 512, 0:w], spread[:], neg_c[:, s:s + w], start=False, stop=(s < PAST))
                mm = pe.matmul(ps[0:64, 4, 0:TQ], keep.ident[0:64, 0:64], new_mask[:], start=False, stop=True)
                mm.then_inc(scores_ready, 1)
                pe.wait_ge(hid_saved, 2 * b + 2)
                compressed_kv(pe, cw, ps[:, 6, :]).then_inc(kcvc_ready, 1)
                for half in range(2):
                    turn(f"slc{half}", [(P, (j * P, (j + 1) * P), kv_slc[:, 4 * half + j, 0:P]) for j in range(4)])
                turn("slc_new", [(P, (0, TQ), new_nsa[:, 256:384])])
                turn("win", [(P, (j * P, (j + 1) * P), kv_win[:, j, 0:P]) for j in range(4)])
                turn("win_new", [(P, (0, TQ), new_win[:, 0:P])])
                saved(TURNS.index("win"))
                saved(TURNS.index("win_new"))
                pe.wait_ge(kcvc_saved, 2 * b + 2)
                for s, w in split(WINDOW + TQ):
                    mm = pe.matmul(ps[0:64, 5 + s // 512, 0:w], q_nsa[:], k_winT[:, s:s + w], start=True, stop=True)
                mm.then_inc(scores_ready, 1)
                pe.matmul(ps[0:64, 7, 0:CMP_N], q_nsa[:], kcT[:, 0:CMP_N], start=True, stop=True).then_inc(scores_ready, 1)
                pe.wait_ge(logits_ready, 4 * b + F + 1)
                for s, w in split(KEYS):
                    mm = pe.matmul(ps[0:64, 2 + s // 512, 0:w], q_nsa[:], k_slcT[:, s:s + w], start=True, stop=True)
                mm.then_inc(scores_ready, 1)

                def turn_probs(name, src, n):
                    turn(name, [(P, (j * 64, (j + 1) * 64), src[:, j * P:(j + 1) * P]) for j in range(n)])

                pe.wait_ge(scaled, 5 * b + 1)
                turn_probs("p_fox", p_fox, 8)
                turn("p_fox_new", [(TQ, (0, 64), p_fox[:, PAST:KEYS])])
                saved(TURNS.index("p_fox"))
                saved(TURNS.index("p_fox_new"))
                pe.wait_ge(logits_ready, 4 * b + W + 1)
                for c in range(4):
                    for j in range(9):
                        kk = P if j < 8 else TQ
                        v = v_fox[:, j, c * P:(c + 1) * P] if j < 8 else new_fox[:, FW + c * P:FW + (c + 1) * P]
                        mm = pe.matmul(ps[:, 5, c * 16:(c + 1) * 16], v, pT_fox[0:kk, j, c * 16:(c + 1) * 16],
                                       start=(j == 0), stop=(j == 8))
                mm.then_inc(out_ready, 1)
                pe.wait_ge(scaled, 5 * b + 2)
                turn("p_cmp", [(CMP_N, (0, 64), p_cmp_n[:, 0:CMP_N])])
                saved(TURNS.index("p_cmp"))
                pe.sem_inc(pe_noted, 1)
                pe.matmul(ps[0:64, 7, 64:81], pT_cmp[0:CMP_N, :], overlap[:], start=True, stop=True).then_inc(imp_ready, 1)
                pe.wait_ge(imp_saved, b + 1)
                pe.sem_inc(pe_noted, 1)
                pe.matmul(ps[0:64, 7, 96:113], same[:], importance[:], start=True, stop=True).then_inc(imp_ready, 1)
                pe.wait_ge(scaled, 5 * b + 4)
                turn_probs("p_win", p_win, 4)
                turn("p_gated", [(CMP_N, (0, 64), p_cmp_g[:, 0:CMP_N])])
                turn("p_win_new", [(TQ, (0, 64), p_win[:, WINDOW:WINDOW + TQ])])
                pe.wait_ge(scaled, 5 * b + 5)
                turn_probs("p_slc", p_slc, 8)
                turn("p_slc_new", [(TQ, (0, 64), p_slc[:, PAST:KEYS])])
                saved(NTURN - 2)
                saved(NTURN - 1)
                parts = [(vc[0:CMP_N, :], pT_gated[0:CMP_N, :])]
                parts += [(kv_win[:, j, P:2 * P], pT_win[:, j, :]) for j in range(4)]
                parts += [(new_win[:, P:2 * P], pT_win[0:TQ, 4, :])]
                parts += [(kv_slc[:, j, P:2 * P], pT_slc[:, j, :]) for j in range(8)]
                parts += [(new_nsa[:, 384:512], pT_slc[0:TQ, 8, :])]
                for n, (v, pt) in enumerate(parts):
                    mm = pe.matmul(ps[:, 6, 0:64], v, pt, start=(n == 0), stop=(n == len(parts) - 1))
                mm.then_inc(out_ready, 1)
                assert state["n"] == NTURN

        @block.scalar
        def _(act):
            act.wait_ge(pb_ready, 1)
            nc.scalar.copy(cw.bias[:], ps[:, 7, 0:2]).then_inc(pb_saved, 1)
            act.wait_ge(pb_saved, 1)
            with act.Fori(0, NREQ) as b:
                def save(name, dst, src, scale=1.0):
                    n = TURNS.index(name)
                    assert n % 2 == 0
                    act.wait_ge(turned, NTURN * b + NTURN + n + 1)
                    nc.scalar.activation(dst, src, ACT.Copy, scale=scale).then_inc(act_saved, 1)

                def exps(j, probs, w):
                    act.wait_ge(logits_ready, 4 * b + j + 1)
                    nc.scalar.activation(probs[:, 0:w], probs[:, 0:w], ACT.Exp, bias=nmax[:, j:j + 1], scale=-1.0,
                                         accum_out=sums[:, j:j + 1]).then_inc(probs_ready, 1)

                four = ps[:, 0, :].rearrange("p (c n) -> p c n", c=4)
                save("logf0", neg_c[:, 0:512], ps[0:8, 0, :], scale=-1.0)
                for p in range(0, NPAGE, 2):
                    save(f"fox{p}", k_foxT[:, :, p * P:(p + 1) * P], four)
                for c in (0, 2):
                    save(f"raw{c}", cw.rawT[:, c, :], ps[:, 0, :])
                act.wait_ge(hid_ready, b + 1)
                for kv in range(2):
                    nc.scalar.activation(cw.hid[:, kv].rearrange("p h n -> p (h n)"),
                                         ps[:, 5, kv * 2 * CMP_N:(kv + 1) * 2 * CMP_N], ACT.Gelu_apprx_tanh,
                                         bias=cw.bias[:, kv:kv + 1]).then_inc(hid_saved, 1)
                save("fox_new", k_foxT[:, :, PAST:KEYS], ps[:, 0, 0:4 * TQ].rearrange("p (c n) -> p c n", c=4))
                exps(F, p_fox, KEYS)
                save("slc1", k_slcT[:, 512:1024], ps[:, 0, :])
                save("win", k_winT[:, 0:512], ps[:, 0, :])
                exps(W, p_win, WINDOW + TQ)
                exps(C, p_cmp, CMP_N)
                save("p_fox", pT_fox[:, 0:8, :], ps[:, 0, :].rearrange("p (j n) -> p j n", j=8))
                save("p_cmp", pT_cmp[0:CMP_N, :], ps[0:CMP_N, 0, 0:64])
                save("p_gated", pT_gated[0:CMP_N, :], ps[0:CMP_N, 0, 0:64])
                exps(S, p_slc, KEYS)
                save("p_slc", pT_slc[:, 0:8, :], ps[:, 0, :].rearrange("p (j n) -> p j n", j=8))

        @block.vector
        def _(dve):
            dve.sem_inc(out_saved, 2)
            dve.wait_ge(ready_in, 16 * (5 + 16 + 8))
            dve.wait_ge(set_ready, 4)
            STEPS = 15
            with dve.Fori(0, NREQ) as b:
                state = {"n": 0}

                def step(ins):
                    state["n"] += 1
                    ins.then_inc(dve_step, 1)
                    dve.wait_ge(dve_step, STEPS * b + state["n"])

                def save(name, dst, src):
                    n = TURNS.index(name)
                    assert n % 2 == 1
                    dve.wait_ge(turned, NTURN * b + NTURN + n + 1)
                    nc.vector.tensor_copy(dst, src).then_inc(dve_saved, 1)

                def logits(j, dst, scores, bias):
                    dve.wait_ge(scores_ready, 4 * b + j + 1)
                    dve.sem_inc(dve_noted, 1)
                    nc.vector.tensor_tensor_reduce(dst, scores, bias, -1.0, FLOOR, ALU.add, ALU.min,
                                                   nmax[:, j:j + 1]).then_inc(logits_ready, 1)

                def over_sum(j, gate=None):
                    dve.wait_ge(probs_ready, 4 * b + j + 1)
                    c = coef[:, j:j + 1]
                    step(nc.vector.tensor_scalar(c, sums[:, j:j + 1], TINY, None, ALU.max))
                    step(nc.vector.reciprocal(c, c))
                    if gate is not None:
                        step(nc.vector.tensor_tensor(c, c, gates[:, bass.ds(b, 1), gate:gate + 1].rearrange("p o j -> p (o j)"), ALU.mult))

                tok = bass.ds(T + b * TQ, TQ)
                for h in range(2):
                    rows = slice(h * HD, (h + 1) * HD)
                    nc.vector.tensor_copy(q_nsa[rows, h * 32:(h + 1) * 32].rearrange("p (g t) -> p g t", t=TQ), keep.qT[rows, :, tok])
                    nc.vector.tensor_copy(q_fox[rows, :].rearrange("p (c x) -> p c x", c=4)[:, :, h * 8:h * 8 + 8],
                                          keep.qfT[rows, :, tok]).then_inc(queries_ready, 1)
                nc.vector.tensor_scalar(neg_c[:, PAST:KEYS], keep.logfT[:, tok], -1.0, None, ALU.mult)
                n1 = TURNS.index("logf1")
                dve.wait_ge(turned, NTURN * b + NTURN + n1 + 1)
                nc.vector.tensor_scalar(neg_c[:, 512:1024], ps[0:8, 1, :], -1.0, None, ALU.mult).then_inc(dve_saved, 1)
                dve.wait_ge(dve_saved, (NTURN // 2) * b + 1)
                dve.wait_ge(act_saved, (NTURN // 2) * b + 1)
                nc.vector.tensor_tensor_scan(neg_c[:], one[:].broadcast_to([8, KEYS]), neg_c[:], 0.0, ALU.mult, ALU.add).then_inc(neg_c_ready, 1)
                for p in range(1, NPAGE, 2):
                    save(f"fox{p}", k_foxT[:, :, p * P:(p + 1) * P], ps[:, 1, :].rearrange("p (c n) -> p c n", c=4))
                for c in (1, 3):
                    save(f"raw{c}", cw.rawT[:, c, :], ps[:, 1, :])
                logits(F, p_fox[:], bank[0:64, 2 * 512:2 * 512 + KEYS], zero[:].broadcast_to([64, KEYS]))
                dve.wait_ge(kcvc_ready, b + 1)
                nc.vector.tensor_copy(kcT[:, 0:CMP_N], ps[:, 6, 0:CMP_N]).then_inc(kcvc_saved, 1)
                nc.vector.tensor_copy(vc[0:CMP_N, :], ps[0:CMP_N, 6, HD:HD + P]).then_inc(kcvc_saved, 1)
                save("slc0", k_slcT[:, 0:512], ps[:, 1, :])
                save("slc_new", k_slcT[:, PAST:KEYS], ps[:, 1, 0:TQ])
                save("win_new", k_winT[:, WINDOW:WINDOW + TQ], ps[:, 1, 0:TQ])
                logits(W, p_win[:], bank[0:64, 5 * 512:5 * 512 + WINDOW + TQ], bias_win[:])
                logits(C, p_cmp[:, 0:CMP_N], ps[0:64, 7, 0:CMP_N], bias_slc[:, 31:31 + 16 * (CMP_N - 1) + 1:16])
                over_sum(F)
                nc.vector.tensor_scalar(p_fox[:], p_fox[:], coef[:, F:F + 1], None, ALU.mult).then_inc(scaled, 1)
                save("p_fox_new", pT_fox[0:TQ, 8, :], ps[0:TQ, 1, 0:64])
                over_sum(C)
                nc.vector.tensor_scalar(p_cmp_n[:, 0:CMP_N], p_cmp[:, 0:CMP_N], coef[:, C:C + 1], None, ALU.mult).then_inc(scaled, 1)
                dve.wait_ge(scaled, 5 * b + 2)
                nc.vector.tensor_scalar(p_cmp_g[:, 0:CMP_N], p_cmp_n[:, 0:CMP_N],
                                        gates[:, bass.ds(b, 1), CMP:CMP + 1].rearrange("p o j -> p (o j)"), None, ALU.mult).then_inc(scaled, 1)
                over_sum(W, WIN)
                nc.vector.tensor_scalar(p_win[:], p_win[:], coef[:, W:W + 1], None, ALU.mult).then_inc(scaled, 1)
                dve.wait_ge(out_ready, 2 * b + 3)
                dve.sem_inc(dve_noted, 1)
                for h in range(2):
                    rows = slice(h * HD, (h + 1) * HD)
                    ins = nc.vector.tensor_copy(keep.qfT[rows, :, tok],
                                                ps[rows, 5, 0:64].rearrange("p (c x) -> p c x", c=4)[:, :, h * 8:h * 8 + 8])
                ins.then_inc(out_saved, 1)
                dve.wait_ge(imp_ready, 2 * b + 1)
                nc.vector.tensor_copy(importance[:], ps[0:64, 7, 64:81]).then_inc(imp_saved, 1)
                dve.wait_ge(imp_ready, 2 * b + 2)
                step(nc.vector.tensor_reduce(pick[:, 15:16], ps[0:64, 7, 97:111], mybir.AxisListType.X, ALU.min))
                step(nc.vector.scalar_tensor_tensor(out=pick[:, 1:15], in0=ps[0:64, 7, 97:111], scalar=pick[:, 15:16],
                                                    in1=block_no[:, 1:15], op0=ALU.is_le, op1=ALU.mult))
                step(nc.vector.tensor_reduce(pick[:, 0:1], pick[:, 1:15], mybir.AxisListType.X, ALU.max))
                step(nc.vector.tensor_scalar(block_mask[:], block_no[:], pick[:, 0:1], NEG, ALU.is_equal, ALU.mult))
                dve.wait_ge(turned, NTURN * b + NTURN + TURNS.index("p_fox_new") + 1)
                nc.vector.tensor_copy(p_slc[:, PAST:KEYS], bias_slc[:, PAST:KEYS])
                step(nc.vector.tensor_tensor(p_slc[:, 0:PAST].rearrange("p (j n) -> p j n", n=SEL),
                                             bias_slc[:, 0:PAST].rearrange("p (j n) -> p j n", n=SEL),
                                             block_mask[:].rearrange("p (j o) -> p j o", o=1).broadcast_to([64, 16, SEL]), ALU.add))
                logits(S, p_slc[:], bank[0:64, 2 * 512:2 * 512 + KEYS], p_slc[:])
                save("p_win", pT_win[:, 0:4, :], ps[:, 1, 0:256].rearrange("p (j n) -> p j n", j=4))
                save("p_win_new", pT_win[0:TQ, 4, :], ps[0:TQ, 1, 0:64])
                over_sum(S, SLC)
                nc.vector.tensor_scalar(p_slc[:], p_slc[:], coef[:, S:S + 1], None, ALU.mult).then_inc(scaled, 1)
                save("p_slc_new", pT_slc[0:TQ, 8, :], ps[0:TQ, 1, 0:64])
                dve.wait_ge(out_ready, 2 * b + 4)
                dve.sem_inc(dve_noted, 1)
                for h in range(2):
                    rows = slice(h * HD, (h + 1) * HD)
                    ins = nc.vector.tensor_copy(keep.qT[rows, :, tok],
                                                ps[rows, 6, h * 32:(h + 1) * 32].rearrange("p (g t) -> p g t", t=TQ))
                ins.then_inc(out_saved, 1)
                assert state["n"] == STEPS


def merge_branches(k, keep, io):
    nc, ps, bank = k.nc, k.ps, k.bank
    with ExitStack() as local:
        def sb(name, shape):
            return local.enter_context(nc.sbuf_tensor(name, shape, F32))

        w_gate = [sb(f"w_gate{e}", [P, 2, KD, P]) for e in range(2)]
        w_branch = [sb(f"w_branch{e}", [P, 2, 4, P]) for e in range(2)]
        sig = sb("sig", [P, 2, 2, 512])
        part = sb("part", [P, 2, 512])
        w_there = k.sems("merge_w0_in", "merge_w1_in")
        products, sig_done, half_done, merged = k.sems("merge_products", "merge_sig", "merge_half", "merged_done")
        w_in = io["w_in"][0].rearrange("(k p) f -> p k f", p=P)
        w_a = io["w_branch_a"][0].rearrange("(h g d) f -> h d g f", h=NKVH, d=HD)
        w_b = io["w_branch_b"][0].rearrange("(c p) f -> p c f", p=P)
        block = local.enter_context(nc.Block())

        @block.sync
        def _(sp):
            with sp.Fori(0, KD // 2) as c2:
                for e in range(2):
                    cols = bass.ds((2 * c2 + e) * P, P)
                    sp.wait_ge(merged, 6 * c2 + 3 * e + 3)
                    sp.dma_start(w_gate[e][:, 0], w_in[:, :, bass.ds(C_GA + (2 * c2 + e) * P, P)]).then_inc(w_there[e], 16)
                    sp.dma_start(w_gate[e][:, 1], w_in[:, :, bass.ds(C_GB + (2 * c2 + e) * P, P)]).then_inc(w_there[e], 16)
                    for h in range(NKVH):
                        sp.dma_start(w_branch[e][h * HD:(h + 1) * HD, 0], w_a[h][:, :, cols]).then_inc(w_there[e], 16)
                    sp.dma_start(w_branch[e][:, 1], w_b[:, :, cols]).then_inc(w_there[e], 16)

        @block.tensor
        def _(pe):
            with pe.Fori(0, KD // 2) as c2:
                for e in range(2):
                    pe.wait_ge(w_there[e], 80 * c2 + 80)
                    for b, (t0, n) in enumerate(BLOCKS):
                        j = 3 * e + b
                        pe.wait_ge(merged, 6 * c2 + j + 5)
                        for side, o in ((0, keep.qT), (1, keep.qfT)):
                            for c in range(KD):
                                pe.matmul(ps[:, 4 * (j % 2) + side, 0:n], w_gate[e][:, side, c, :], keep.xT[:, c, t0:t0 + n],
                                          start=(c == 0), stop=(c == KD - 1))
                            for c in range(4):
                                mm = pe.matmul(ps[:, 4 * (j % 2) + 2 + side, 0:n], w_branch[e][:, side, c, :], o[:, c, t0:t0 + n],
                                               start=(c == 0), stop=(c == 3))
                        mm.then_inc(products, 1)

        @block.scalar
        def _(act):
            with act.Fori(0, KD // 2) as c2:
                for j in range(6):
                    n = BLOCKS[j % 3][1]
                    act.wait_ge(products, 6 * c2 + j + 1)
                    nc.scalar.activation(sig[:, j % 2, :, 0:n], ps[:, 4 * (j % 2):4 * (j % 2) + 2, 0:n],
                                         ACT.Sigmoid).then_inc(sig_done, 1)

        @block.vector
        def _(dve):
            dve.sem_inc(merged, 6)
            with dve.Fori(0, KD // 2) as c2:
                for j in range(6):
                    t0, n = BLOCKS[j % 3]
                    q = 4 * (j % 2)
                    dve.wait_ge(sig_done, 6 * c2 + j + 1)
                    dve.wait_ge(merged, 6 * c2 + j + 6)
                    nc.vector.tensor_tensor(part[:, :, 0:n], sig[:, j % 2, :, 0:n], ps[:, q + 2:q + 4, 0:n],
                                            ALU.mult).then_inc(half_done, 1)
                    dve.wait_ge(half_done, 6 * c2 + j + 1)
                    nc.vector.tensor_tensor(keep.mergedT[:, bass.ds(2 * c2 + j // 3, 1), t0:t0 + n].rearrange("p o n -> p (o n)"),
                                            part[:, 0, 0:n], part[:, 1, 0:n], ALU.add).then_inc(merged, 1)


def add_product(k, io, tag, weights, kk, src, res):
    nc, ps, bank = k.nc, k.ps, k.bank
    with ExitStack() as local:
        w = [local.enter_context(nc.sbuf_tensor(f"w_{tag}{e}", [P, kk, P], F32)) for e in range(2)]
        w_there = k.sems(f"{tag}_w0_in", f"{tag}_w1_in")
        product, added = k.sems(f"{tag}_product", f"{tag}_added")
        w_dram = weights.rearrange("(k p) f -> p k f", p=P)
        block = local.enter_context(nc.Block())

        @block.sync
        def _(sp):
            with sp.Fori(0, KD // 2) as c2:
                for e in range(2):
                    sp.wait_ge(added, 6 * c2 + 3 * e + 3)
                    sp.dma_start(w[e][:], w_dram[:, :, bass.ds((2 * c2 + e) * P, P)]).then_inc(w_there[e], 16)

        @block.tensor
        def _(pe):
            with pe.Fori(0, KD // 2) as c2:
                for e in range(2):
                    pe.wait_ge(w_there[e], 16 * c2 + 16)
                    for b, (t0, n) in enumerate(BLOCKS):
                        pe.wait_ge(added, 6 * c2 + 3 * e + b + 1)
                        for c in range(kk):
                            mm = pe.matmul(ps[:, 3 * e + b, 0:n], w[e][:, c, :], src[:, c, t0:t0 + n],
                                           start=(c == 0), stop=(c == kk - 1))
                        mm.then_inc(product, 1)

        @block.vector
        def _(dve):
            dve.sem_inc(added, 6)
            with dve.Fori(0, KD // 2) as c2:
                for j in range(6):
                    t0, n = BLOCKS[j % 3]
                    r = res[:, bass.ds(2 * c2 + j // 3, 1), t0:t0 + n].rearrange("p o n -> p (o n)")
                    dve.wait_ge(product, 6 * c2 + j + 1)
                    nc.vector.scalar_tensor_tensor(out=r, in0=r, scalar=ALPHA, in1=ps[:, j, 0:n],
                                                   op0=ALU.mult, op1=ALU.add).then_inc(added, 1)


def normalise(k, io, tag, gain, shift, r):
    nc, ps, bank = k.nc, k.ps, k.bank
    with ExitStack() as local:
        def sb(name, shape):
            return local.enter_context(nc.sbuf_tensor(f"{tag}_{name}", shape, F32))

        mean_of, eps = sb("mean_of", [P, P]), sb("eps", [P, 1])
        g, s = sb("g", [P, KD]), sb("s", [P, KD])
        squares, rstd = sb("squares", [P, KD, 512]), sb("rstd", [P, 3, 512])
        set_up, gs_in, mean_ready, centred, squared, var_ready, std_done, rstd_done, scaled, done = k.sems(*(
            f"{tag}_{x}" for x in ("set_up", "gs_in", "mean_ready", "centred", "squared", "var_ready", "std_done",
                                   "rstd_done", "scaled", "done")))
        PARTS = 4
        block = local.enter_context(nc.Block())

        @block.sync
        def _(sp):
            for dst, src in ((g, gain), (s, shift)):
                sp.dma_start(dst[:], src.rearrange("(k p) -> p k", p=P), allow_slow_non_contiguous=True).then_inc(gs_in, 16)

        @block.gpsimd
        def _(pool):
            nc.gpsimd.memset(mean_of[:], 1.0 / D).then_inc(set_up, 1)
            nc.gpsimd.memset(eps[:], EPS).then_inc(set_up, 1)

        @block.tensor
        def _(pe):
            pe.wait_ge(set_up, 2)
            for b, (t0, n) in enumerate(BLOCKS):
                for c in range(KD):
                    mm = pe.matmul(ps[:, b, 0:n], mean_of[:], r[:, c, t0:t0 + n], start=(c == 0), stop=(c == KD - 1))
                mm.then_inc(mean_ready, 1)
            for b, (t0, n) in enumerate(BLOCKS):
                for c in range(KD):
                    if c % 2 == 0:
                        pe.wait_ge(squared, PARTS * b + c // 2 + 1)
                    mm = pe.matmul(ps[:, 3 + b, 0:n], mean_of[:], squares[:, c, 0:n], start=(c == 0), stop=(c == KD - 1))
                mm.then_inc(var_ready, 1)

        @block.scalar
        def _(act):
            def square(b, q):
                t0, n = BLOCKS[b]
                act.wait_ge(centred, PARTS * b + q + 1)
                if b:
                    act.wait_ge(var_ready, b)
                nc.scalar.activation(squares[:, 2 * q:2 * q + 2, 0:n], r[:, 2 * q:2 * q + 2, t0:t0 + n],
                                     ACT.Square).then_inc(squared, 1)

            for b in range(3):
                for q in range(PARTS):
                    square(b, q)
            act.wait_ge(gs_in, 32)
            for b, (t0, n) in enumerate(BLOCKS):
                act.wait_ge(var_ready, b + 1)
                nc.scalar.activation(rstd[:, b, 0:n], ps[:, 3 + b, 0:n], ACT.Sqrt, bias=eps[:]).then_inc(std_done, 1)
            for b, (t0, n) in enumerate(BLOCKS):
                for c in range(KD):
                    if c % 2 == 0:
                        act.wait_ge(scaled, PARTS * b + c // 2 + 1)
                    nc.scalar.activation(r[:, c, t0:t0 + n], r[:, c, t0:t0 + n], ACT.Identity, bias=s[:, c:c + 1],
                                         scale=g[:, c:c + 1]).then_inc(done, 1)

        @block.vector
        def _(dve):
            for b, (t0, n) in enumerate(BLOCKS):
                dve.wait_ge(mean_ready, b + 1)
                for q in range(PARTS):
                    x = r[:, 2 * q:2 * q + 2, t0:t0 + n]
                    nc.vector.tensor_tensor(x, x, ps[:, b:b + 1, 0:n].broadcast_to([P, 2, n]), ALU.subtract).then_inc(centred, 1)
            for b, (t0, n) in enumerate(BLOCKS):
                dve.wait_ge(std_done, b + 1)
                nc.vector.reciprocal(rstd[:, b, 0:n], rstd[:, b, 0:n]).then_inc(rstd_done, 1)
                dve.wait_ge(rstd_done, b + 1)
                dve.wait_ge(squared, PARTS * (b + 1))
                for q in range(PARTS):
                    x = r[:, 2 * q:2 * q + 2, t0:t0 + n]
                    nc.vector.tensor_tensor(x, x, rstd[:, b:b + 1, 0:n].broadcast_to([P, 2, n]), ALU.mult).then_inc(scaled, 1)


def gated_ffn(k, keep, io):
    nc, ps, bank = k.nc, k.ps, k.bank
    x = keep.xT
    TAIL = 2 + 2 * NREQ
    with ExitStack() as local:
        def sb(name, shape):
            return local.enter_context(nc.sbuf_tensor(name, shape, F32))

        w_ug = [sb(f"w_ug{e}", [P, 2, KD, P]) for e in range(2)]
        up = [sb(f"up{e}", [P, 2 + T]) for e in range(2)]
        up_r = [sb(f"up_r{e}", [P, NREQ, 2 + TQ]) for e in range(2)]
        conv = sb("conv", [P, 3, 512])
        taps = sb("taps", [P, 4, NFF])
        cur = [sb(f"cur_taps{e}", [P, 4]) for e in range(2)]
        prev = sb("prev", [2 * NREQ, DFF])
        prevT = sb("prevT", [P, NFF, 2 * NREQ])
        tail = [sb(f"tail{e}", [P, TAIL]) for e in range(2)]
        tail_rows = sb("tail_rows", [TAIL, DFF])
        w_there = k.sems("ug_w0_in", "ug_w1_in")
        (taps_in, prev_in, prev_turned, prevT_saved, zeroed, chunk_set, products, up_saved, conv_step, conv_ready,
         gelu_done, h_done, tail_set, tail_turned, tail_saved, tail_out,
         pool_noted) = k.sems(
            "taps_in", "prev_in", "prev_turned", "prevT_saved", "zeroed", "chunk_set", "ug_products", "up_saved",
            "conv_step", "conv_ready", "gelu_done", "h_done", "tail_set", "tail_turned", "tail_saved", "tail_out",
            "pool_noted")
        w_up = io["w_ffn_up"][0].rearrange("(k p) f -> p k f", p=P)
        w_gate = io["w_ffn_gate"][0].rearrange("(k p) f -> p k f", p=P)
        block = local.enter_context(nc.Block())

        @block.sync
        def _(sp):
            sp.dma_start(prev[:], io["state_ffn_conv"][0].rearrange("b k f -> (b k) f")).then_inc(prev_in, 16)
            for n in range(3):
                sp.dma_start(taps[:, n, :], io["ffn_conv_w"][0, n].rearrange("(c p) -> p c", p=P), allow_slow_non_contiguous=True).then_inc(taps_in, 16)
            sp.dma_start(taps[:, 3, :], io["ffn_conv_b"][0].rearrange("(c p) -> p c", p=P), allow_slow_non_contiguous=True).then_inc(taps_in, 16)
            with sp.Fori(0, NFF // 2) as c2:
                for e in range(2):
                    cols = bass.ds((2 * c2 + e) * P, P)
                    sp.wait_ge(h_done, 6 * c2 + 3 * e + 3)
                    sp.dma_start(w_ug[e][:, 0], w_up[:, :, cols]).then_inc(w_there[e], 16)
                    sp.dma_start(w_ug[e][:, 1], w_gate[:, :, cols]).then_inc(w_there[e], 16)
            sp.wait_ge(tail_saved, NFF + 1)
            sp.dma_start(io["o_conv_prompt"], tail_rows[0:2, :]).then_inc(tail_out, 16)
            sp.dma_start(io["o_conv_sample"], tail_rows[2:TAIL, :]).then_inc(tail_out, 16)
            sp.wait_ge(tail_out, 32)

        @block.gpsimd
        def _(pool):
            for e in range(2):
                nc.gpsimd.memset(up[e][:, 0:2], 0.0).then_inc(zeroed, 1)
            pool.sem_inc(tail_set, 4)
            pool.wait_ge(prevT_saved, 1)
            pool.wait_ge(taps_in, 64)
            with pool.Fori(0, NFF // 2) as c2:
                for e in range(2):
                    chunk = bass.ds(2 * c2 + e, 1)
                    pool.wait_ge(h_done, 6 * c2 + 3 * e + 3)
                    nc.gpsimd.tensor_copy(cur[e][:], taps[:, :, chunk].rearrange("p a o -> p (a o)")).then_inc(chunk_set, 1)
                    nc.gpsimd.tensor_copy(up_r[e][:, :, 0:2], prevT[:, chunk, :].rearrange("p o (b r) -> p (o b) r", r=2)).then_inc(chunk_set, 1)
                for e in range(2):
                    pool.wait_ge(up_saved, 6 * c2 + 3 * e + 3)
                    pool.wait_ge(tail_turned, 2 * c2 + e + 1)
                    pool.sem_inc(pool_noted, 1)
                    nc.gpsimd.tensor_copy(tail[e][:, 0:2], up[e][:, T:T + 2]).then_inc(tail_set, 1)
                    nc.gpsimd.tensor_copy(tail[e][:, 2:TAIL].rearrange("p (b r) -> p b r", r=2), up_r[e][:, :, TQ:TQ + 2]).then_inc(tail_set, 1)

        @block.tensor
        def _(pe):
            pe.sem_inc(tail_turned, 2)
            pe.wait_ge(prev_in, 16)
            for c in range(NFF):
                mm = pe.transpose(ps[:, 6, c * 16:(c + 1) * 16], prev[:, c * P:(c + 1) * P], keep.ident[0:16, 0:16])
            mm.then_inc(prev_turned, 1)
            with pe.Fori(0, NFF // 2) as c2:
                for e in range(2):
                    pe.wait_ge(w_there[e], 32 * c2 + 32)
                    for b, (t0, n) in enumerate(FFN_BLOCKS):
                        j = 3 * e + b
                        pe.wait_ge(h_done, 6 * c2 + j + 4)
                        for side in range(2):
                            for c in range(KD):
                                mm = pe.matmul(ps[:, 2 * (j % 3) + side, 0:n], w_ug[e][:, side, c, :], x[:, c, t0:t0 + n],
                                               start=(c == 0), stop=(c == KD - 1))
                        mm.then_inc(products, 1)
                for e in range(2):
                    pe.wait_ge(tail_set, 4 * c2 + 2 * e + 6)
                    pe.wait_ge(tail_saved, 2 * c2 + e + 1)
                    pe.transpose(ps[0:TAIL, 7, 0:P], tail[e][:], keep.ident[:]).then_inc(tail_turned, 1)

        @block.scalar
        def _(act):
            act.wait_ge(prev_turned, 1)
            nc.scalar.copy(prevT[:].rearrange("p c r -> p (c r)"), ps[:, 6, 0:16 * NFF]).then_inc(prevT_saved, 1)
            act.sem_inc(tail_saved, 1)
            act.wait_ge(zeroed, 2)
            with act.Fori(0, NFF // 2) as c2:
                def save(j):
                    act.wait_ge(products, 6 * c2 + j + 1)
                    act.wait_ge(h_done, 6 * c2 + j + 2)
                    if j % 3 == 0:
                        act.wait_ge(tail_set, 4 * c2 + 2 * (j // 3) + 2)
                    b, src, (t0, n) = j % 3, ps[:, 2 * (j % 3), :], FFN_BLOCKS[j % 3]
                    if b < 2:
                        nc.scalar.copy(up[j // 3][:, 2 + t0:2 + t0 + n], src[:, 0:n]).then_inc(up_saved, 1)
                    else:
                        nc.scalar.copy(up[j // 3][:, 2 + t0:2 + T], src[:, 0:T - t0])
                        nc.scalar.copy(up_r[j // 3][:, :, 2:2 + TQ], src[:, T - t0:n].rearrange("p (b t) -> p b t", t=TQ)).then_inc(up_saved, 1)

                def gelu(j):
                    n = FFN_BLOCKS[j % 3][1]
                    act.wait_ge(conv_ready, 6 * c2 + j + 1)
                    nc.scalar.activation(conv[:, j % 3, 0:n], conv[:, j % 3, 0:n], ACT.Gelu_apprx_tanh).then_inc(gelu_done, 1)

                for j in range(6):
                    save(j)
                    gelu(j)
                for e in range(2):
                    act.wait_ge(tail_turned, 2 * c2 + e + 3)
                    nc.scalar.copy(tail_rows[:, bass.ds((2 * c2 + e) * P, P)], ps[0:TAIL, 7, 0:P]).then_inc(tail_saved, 1)

        @block.vector
        def _(dve):
            dve.sem_inc(h_done, 6)
            with dve.Fori(0, NFF // 2) as c2:
                for j in range(6):
                    e, (t0, n) = j // 3, FFN_BLOCKS[j % 3]
                    dve.wait_ge(up_saved, 6 * c2 + j + 1)
                    if j % 3 == 0:
                        dve.wait_ge(chunk_set, 4 * c2 + 2 * e + 2)
                    m = min(n, T - t0)
                    parts = [([up[e][:, t0 + a:t0 + a + m] for a in range(3)], conv[:, j % 3, 0:m])]
                    if m < n:
                        parts.append(([up_r[e][:, :, a:a + TQ] for a in range(3)],
                                      conv[:, j % 3, m:n].rearrange("p (b t) -> p b t", t=TQ)))
                    base = 12 * c2 + 2 * j
                    for rows, c in parts:
                        ins = nc.vector.tensor_scalar(c, rows[0], cur[e][:, 0:1], cur[e][:, 3:4], ALU.mult, ALU.add)
                    ins.then_inc(conv_step, 1)
                    dve.wait_ge(conv_step, base + 1)
                    for rows, c in parts:
                        ins = nc.vector.scalar_tensor_tensor(out=c, in0=rows[1], scalar=cur[e][:, 1:2], in1=c, op0=ALU.mult, op1=ALU.add)
                    ins.then_inc(conv_step, 1)
                    dve.wait_ge(conv_step, base + 2)
                    for rows, c in parts:
                        ins = nc.vector.scalar_tensor_tensor(out=c, in0=rows[2], scalar=cur[e][:, 2:3], in1=c, op0=ALU.mult, op1=ALU.add)
                    ins.then_inc(conv_ready, 1)
                    dve.wait_ge(gelu_done, 6 * c2 + j + 1)
                    nc.vector.tensor_tensor(keep.hT[:, bass.ds(2 * c2 + e, 1), t0:t0 + n].rearrange("p o n -> p (o n)"),
                                            conv[:, j % 3, 0:n], ps[:, 2 * (j % 3) + 1, 0:n], ALU.mult).then_inc(h_done, 1)


def layer_output(k, keep, io):
    nc, ps, bank = k.nc, k.ps, k.bank
    x = keep.xT
    KP = PLE // P
    with ExitStack() as local:
        def sb(name, shape):
            return local.enter_context(nc.sbuf_tensor(name, shape, F32))

        p_rows = sb("p_rows", [P, NT, PLE])
        pT = sb("pT", [P, KP, RP])
        w_g = [sb(f"w_pg{e}", [P, KD, P]) for e in range(2)]
        w_p = [sb(f"w_pp{e}", [P, KP, P]) for e in range(2)]
        sig = sb("sig_p", [P, 2, 512])
        y = [sb(f"y{e}", [P, R]) for e in range(2)]
        rows = [sb(f"y_rows{e}", [P, NT, P]) for e in range(2)]
        w_there = k.sems("ple_w0_in", "ple_w1_in")
        (p_in, p_turned, p_saved, products, sig_done, half_done, y_done, y_turned, rows_saved, rows_free, stored0, stored1) = k.sems(
            "p_in", "p_turned", "p_saved", "ple_products", "ple_sig", "ple_half", "y_done", "y_turned", "y_saved", "rows_free",
            "stored0", "stored1")
        stored = (stored0, stored1)
        wg = io["w_ple_gate"][0].rearrange("(k p) f -> p k f", p=P)
        wp = io["w_ple"][0].rearrange("(k p) f -> p k f", p=P)
        block = local.enter_context(nc.Block())

        @block.sync
        def _(sp):
            sp.dma_start(p_rows[:], io["p_all"].rearrange("(i p) f -> p i f", p=P)).then_inc(p_in, 16)
            with sp.Fori(0, KD // 2) as c2:
                for e in range(2):
                    cols = bass.ds((2 * c2 + e) * P, P)
                    sp.wait_ge(y_done, 6 * c2 + 3 * e + 3)
                    sp.dma_start(w_g[e][:], wg[:, :, cols]).then_inc(w_there[e], 16)
                    sp.dma_start(w_p[e][:], wp[:, :, cols]).then_inc(w_there[e], 16)

        @block.gpsimd
        def _(pool):
            pool.sem_inc(rows_free, 2)
            with pool.Fori(0, KD // 2) as c2:
                for e in range(2):
                    cols = bass.ds((2 * c2 + e) * P, P)
                    pool.wait_ge(rows_saved, 4 * c2 + 2 * e + 4)
                    pool.dma_start(io["o_y"][0:T, cols].rearrange("(i p) f -> p i f", p=P), rows[e][:, 0:NTP, :]).then_inc(stored[e], 16)
                    pool.dma_start(io["o_y"][T:R, cols], rows[e][0:R - T, NTP, :]).then_inc(stored[e], 16)
                for e in range(2):
                    pool.wait_ge(stored[e], 32 * c2 + 32)
                    pool.sem_inc(rows_free, 1)

        @block.tensor
        def _(pe):
            pe.sem_inc(y_turned, 2)
            pe.wait_ge(p_in, 16)
            for c in range(KP):
                if c:
                    pe.wait_ge(p_saved, c)
                for i in range(NT):
                    mm = pe.transpose(ps[:, 4 + i // 4, (i % 4) * P:(i % 4 + 1) * P], p_rows[:, i, c * P:(c + 1) * P], keep.ident[:])
                mm.then_inc(p_turned, 1)
            pe.wait_ge(p_saved, KP)
            with pe.Fori(0, KD // 2) as c2:
                for e in range(2):
                    pe.wait_ge(w_there[e], 32 * c2 + 32)
                    for b, (t0, n) in enumerate(BLOCKS):
                        j = 3 * e + b
                        pe.wait_ge(y_done, 6 * c2 + j + 5)
                        for c in range(KD):
                            pe.matmul(ps[:, 2 * (j % 2), 0:n], w_g[e][:, c, :], x[:, c, t0:t0 + n], start=(c == 0), stop=(c == KD - 1))
                        for c in range(KP):
                            mm = pe.matmul(ps[:, 2 * (j % 2) + 1, 0:n], w_p[e][:, c, :], pT[:, c, t0:t0 + n], start=(c == 0), stop=(c == KP - 1))
                        mm.then_inc(products, 1)
                    pe.wait_ge(y_done, 6 * c2 + 3 * e + 9)
                    pe.wait_ge(rows_saved, 4 * c2 + 2 * e + 2)
                    for i in range(NT):
                        n = min(P, R - i * P)
                        mm = pe.transpose(ps[0:n, 4 + i // 4, (i % 4) * P:(i % 4 + 1) * P], y[e][:, i * P:i * P + n], keep.ident[:])
                    mm.then_inc(y_turned, 1)

        @block.scalar
        def _(act):
            for c in range(KP):
                act.wait_ge(p_turned, c + 1)
                nc.scalar.copy(pT[:, c, :], bank[:, 4 * 512:4 * 512 + RP]).then_inc(p_saved, 1)
            act.sem_inc(rows_saved, 2)
            with act.Fori(0, KD // 2) as c2:
                for e in range(2):
                    for b in range(3):
                        j, n = 3 * e + b, BLOCKS[b][1]
                        act.wait_ge(products, 6 * c2 + j + 1)
                        nc.scalar.activation(sig[:, j % 2, 0:n], ps[:, 2 * (j % 2), 0:n], ACT.Sigmoid).then_inc(sig_done, 1)
                    act.wait_ge(y_turned, 2 * c2 + e + 3)
                    act.wait_ge(rows_free, 2 * c2 + e + 1)
                    nc.scalar.copy(rows[e][:, 0:NTP, :], ps[:, 4:6, :].rearrange("p b (i f) -> p (b i) f", i=4)).then_inc(rows_saved, 1)
                    nc.scalar.copy(rows[e][0:R - T, NTP, :], ps[0:R - T, 6, 0:P]).then_inc(rows_saved, 1)

        @block.vector
        def _(dve):
            dve.sem_inc(y_done, 6)
            with dve.Fori(0, KD // 2) as c2:
                for j in range(6):
                    e, (t0, n) = j // 3, BLOCKS[j % 3]
                    dve.wait_ge(sig_done, 6 * c2 + j + 1)
                    nc.vector.tensor_tensor(sig[:, j % 2, 0:n], sig[:, j % 2, 0:n], ps[:, 2 * (j % 2) + 1, 0:n], ALU.mult).then_inc(half_done, 1)
                    dve.wait_ge(half_done, 6 * c2 + j + 1)
                    if j % 3 == 0:
                        dve.wait_ge(y_turned, 2 * c2 + e + 1)
                    nc.vector.tensor_tensor(y[e][:, t0:t0 + n], sig[:, j % 2, 0:n],
                                            x[:, bass.ds(2 * c2 + e, 1), t0:t0 + n].rearrange("p o n -> p (o n)"), ALU.add).then_inc(y_done, 1)


class Keep:
    pass


def hybrid_nsa_fox_step(nc, io):
    with ExitStack() as ctx:
        k = Core(nc, io, ctx)
        keep = Keep()
        io["rev"] = k.scratch("rev_dram", (8, 2 * NDIST))
        io["bias_rows"] = k.scratch("bias_rows", (8, P, 2 * NDIST))
        io["neg_sums"] = k.scratch("neg_sums", (8, T))
        io["gate_rows"] = k.scratch("gate_rows", (NREQ * TQ, 24))

        def sb(stack, name, shape):
            return stack.enter_context(nc.sbuf_tensor(name, shape, F32))

        keep.ident = sb(ctx, "ident", [P, P])
        keep.logfT = sb(ctx, "logfT", [8, RP])
        keep.gates = sb(ctx, "gates", [P, NT, 24])
        keep.xT = sb(ctx, "xT", [P, KD, RP])
        mixers = ctx.enter_context(ExitStack())
        keep.qT = sb(mixers, "qT", [P, NG, R])
        keep.qfT = sb(mixers, "qfT", [P, 4, R])
        with ExitStack() as early:
            keep.fkT = sb(early, "fkT", [P, 4, RP])
            keep.keyT = sb(early, "keyT", [P, 2, RP])
            keep.v_slc = sb(early, "v_slc", [P, NT, P])
            keep.v_win = sb(early, "v_win", [P, NT, P])
            keep.fv = sb(early, "fv", [P, NT, FW])
            keep.ff = sb(early, "ff", [P, NT, 8])
            project_rows(k, keep, io)
            forget_and_bias(k, keep, io)
            project_queries(k, keep, io)
            keep.kcT = sb(early, "kcT", [P, 64])
            keep.vc = sb(early, "vc", [64, P])
            compress_prompt(k, keep, io)
            prompt_attention(k, keep, io)
        request_attention(k, keep, io)
        k.recycle()
        keep.mergedT = sb(mixers, "mergedT", [P, KD, R])
        merge_branches(k, keep, io)
        add_product(k, io, "out", io["w_out"][0], KD, keep.mergedT, keep.xT)
        mixers.close()
        normalise(k, io, "ln1", io["ln1_g"][0], io["ln1_b"][0], keep.xT)
        with ExitStack() as ffn:
            keep.hT = sb(ffn, "hT", [P, NFF, R])
            gated_ffn(k, keep, io)
            add_product(k, io, "down", io["w_ffn_down"][0], NFF, keep.hT, keep.xT)
        normalise(k, io, "ln2", io["ln2_g"][0], io["ln2_b"][0], keep.xT)
        layer_output(k, keep, io)


def shape_constants():
    import numpy as np

    def bucket(dist):
        n = np.maximum(dist, 0)
        nf = np.maximum(n, 1).astype(np.float32)
        large = 16 + (np.log(nf / np.float32(16)) / np.float32(np.log(8.0)) * np.float32(16)).astype(np.int32)
        return np.where(n < 16, n, np.minimum(large, 31))

    dist = DIST0 - np.arange(NDIST)
    onehot = np.zeros((33, 2, NDIST), np.float32)
    for w in range(2):
        masked = (dist < 0) | ((dist >= WINDOW) if w else False)
        row = np.where(masked, 32, bucket(dist))
        onehot[row, w, np.arange(NDIST)] = 1.0
    ident = np.eye(P, dtype=np.float32)
    q = np.arange(P)
    causal = np.where(q[None, :] > q[:, None], np.float32(NEG), np.float32(0)).astype(np.float32)
    row = np.arange(64)
    newmask = np.where(np.arange(TQ)[None, :] > (row % 8)[:, None], np.float32(NEG), np.float32(0)).astype(np.float32)
    start = np.arange(CMP_N)[:, None] * 16
    j = np.arange(17)[None, :]
    overlap = ((start < (j + 1) * SEL) & (start + 32 > j * SEL)).astype(np.float32)
    same = ((row[:, None] // 32 == row[None, :] // 32) & (row[:, None] % 8 == row[None, :] % 8)).astype(np.float32)
    spread = (np.arange(8)[:, None] == row[None, :] // 8).astype(np.float32)
    block = np.broadcast_to(np.arange(16, dtype=np.float32), (64, 16)).copy()
    return dict(c_onehot=onehot.reshape(33, 2 * NDIST), c_ident=ident, c_causal=causal, c_newmask=newmask,
                c_overlap=overlap, c_same=same, c_spread=spread, c_block=block)


_OUTS = [("y", (R, D)), ("fox_kv", (RP, 2 * FW)), ("logf", (RP, 8)), ("nsa_kv", (RP, 512)),
         ("win_rows", (RP, 256)), ("win_sample", (NREQ, WINDOW, 256)),
         ("conv_prompt", (2, DFF)), ("conv_sample", (2 * NREQ, DFF))]


def kernel(**inputs):
    import numpy as np
    import concourse.bacc as bacc
    from concourse.bass_utils import run_bass_kernel_spmd as run

    given = {k: np.ascontiguousarray(v) for k, v in inputs.items()}

    def rows(a, b, n):
        a, b = a.reshape(T, -1), b.reshape(NREQ * TQ, -1)
        return np.concatenate([a, b, np.zeros((n - R, a.shape[1]), a.dtype)])

    given["x_all"] = rows(given.pop("x_prompt"), given.pop("x_sample"), RP + P)
    given["p_all"] = rows(given.pop("p_prompt"), given.pop("p_sample"), RP)
    given.update(shape_constants())
    nc = bacc.Bacc("TRN2", target_bir_lowering=False, num_devices=1)
    arrays, args = {}, {}
    for name, a in given.items():
        arrays[f"in_{name}"] = a
        args[name] = nc.dram_tensor(f"in_{name}", a.shape, mybir.dt.from_np(a.dtype), kind="ExternalInput").ap()
    for name, shape in _OUTS:
        args["o_" + name] = nc.dram_tensor(f"out_{name}", shape, F32, kind="ExternalOutput").ap()
    hybrid_nsa_fox_step(nc, args)
    r = run(nc, [arrays], core_ids=[0]).results[0]
    o = {name: r[f"out_{name}"] for name, _ in _OUTS}
    return (
        o["y"][:T].reshape(1, T, D), o["y"][T:].reshape(NREQ, TQ, D),
        o["fox_kv"][:T].reshape(1, 1, T, 2, 8, HD), o["fox_kv"][T:R].reshape(1, NREQ, TQ, 2, 8, HD),
        o["logf"][:T].reshape(1, 1, T, 8), o["logf"][T:R].reshape(1, NREQ, TQ, 8),
        o["nsa_kv"][:T].reshape(1, 1, T, 4, 2, HD), o["nsa_kv"][T:R].reshape(1, NREQ, TQ, 4, 2, HD),
        o["win_rows"][T - WINDOW:T].reshape(1, 1, WINDOW, 2, 2, HD),
        o["win_sample"].reshape(1, NREQ, WINDOW, 2, 2, HD),
        o["conv_prompt"].reshape(1, 1, 2, DFF), o["conv_sample"].reshape(1, NREQ, 2, DFF),
    )
```
